# Optimizing a Trainium2 kernel written in Bass

```python
import jax
import jax.numpy as jnp
from jax import lax
import numpy as np
import math
import jax, jax.numpy as jnp

D_MODEL = 2048
BATCH = 1
SEQ = 256
DEPTH = 1

GRID_W = 64
CTX_LEN = 256
D_MIX = D_MODEL
D_ATTN = D_MIX // 2
D_RWKV = D_MIX - D_ATTN
HEAD_DIM = 64
N_HEADS_A = D_ATTN // HEAD_DIM
N_KV_HEADS = 4
GQA_GROUP = N_HEADS_A // N_KV_HEADS
WINDOW = 128
BLOCK = 128
BAND = BLOCK + 2 * WINDOW
ROPE_BASE = 10000.0
RWKV_HEAD = 64
N_HEADS_R = D_RWKV // RWKV_HEAD
D_DECAY_LORA = max(32, int(round(1.8 * D_RWKV ** 0.5 / 32)) * 32)
D_AAA_LORA = max(32, int(round(1.8 * D_RWKV ** 0.5 / 32)) * 32)
D_GATE_LORA = max(32, int(round(0.6 * D_RWKV ** 0.8 / 32)) * 32)
D_FF = -(-(8 * D_MODEL) // (3 * 256)) * 256
NORM_EPS = 1e-6
LNX_EPS = 64e-5
MASK_VALUE = -1e30
ATTN_SPLITS = (D_ATTN, N_KV_HEADS * HEAD_DIM, N_KV_HEADS * HEAD_DIM)
RWKV_SPLITS = (D_RWKV, D_RWKV, D_RWKV, D_DECAY_LORA, D_DECAY_LORA, D_AAA_LORA, D_AAA_LORA, D_GATE_LORA)
D_IN_ATTN = sum(ATTN_SPLITS)
D_IN_RWKV = sum(RWKV_SPLITS)
D_IN = D_IN_ATTN + D_IN_RWKV
F32 = jnp.float32


def _split(z, sizes):
    return jnp.split(z, [int(s) for s in np.cumsum(sizes)[:-1]], axis=-1)

def rmsnorm(x, g):
    xf = x.astype(F32)
    y = xf * lax.rsqrt(jnp.mean(xf * xf, axis=-1, keepdims=True) + NORM_EPS)
    return (y * g.astype(F32)).astype(x.dtype)

def modulate(h, shift, scale):
    return h * (1 + scale) + shift

def swiglu(h, w1, w3, w2):
    return (jax.nn.silu(h @ w1) * (h @ w3)) @ w2

def axial_rope(x, row, col):
    half = HEAD_DIM // 2
    nf = half // 2
    freqs = 1.0 / (ROPE_BASE ** (jnp.arange(nf, dtype=F32) / nf))

    def rot(xa, pos):
        ang = pos.astype(F32)[:, None] * freqs[None, :]
        cos = jnp.cos(ang)[None, :, None, :]
        sin = jnp.sin(ang)[None, :, None, :]
        x1, x2 = xa[..., :nf], xa[..., nf:]
        return jnp.concatenate([x1 * cos - x2 * sin, x2 * cos + x1 * sin], axis=-1)

    xf = x.astype(F32)
    return jnp.concatenate([rot(xf[..., :half], row), rot(xf[..., half:], col)], axis=-1).astype(x.dtype)

def sink_softmax(s, sink_hg):
    sk = sink_hg[None, :, :, None, None]
    m = jnp.maximum(jnp.max(s, axis=-1, keepdims=True), sk)
    p = jnp.exp(s - m)
    return p / (jnp.sum(p, axis=-1, keepdims=True) + jnp.exp(sk - m))

def windowed_gqa(q, k, v, k_ctx, v_ctx, sink):
    B, T = q.shape[0], q.shape[1]
    nb = T // BLOCK
    scale = HEAD_DIM ** -0.5
    qb = (q.astype(F32) * scale).reshape(B, nb, BLOCK, N_KV_HEADS, GQA_GROUP, HEAD_DIM)
    qb = qb.transpose(1, 0, 2, 3, 4, 5)
    pad = ((0, 0), (WINDOW, WINDOW), (0, 0), (0, 0))
    kp = jnp.pad(k.astype(F32), pad)
    vp = jnp.pad(v.astype(F32), pad)
    kc = k_ctx.astype(F32)
    vc = v_ctx.astype(F32)
    sink_hg = sink.astype(F32).reshape(N_KV_HEADS, GQA_GROUP)
    offs_q = jnp.arange(BLOCK)
    offs_k = jnp.arange(BAND) - WINDOW
    in_window = jnp.abs(offs_q[:, None] - offs_k[None, :]) <= WINDOW

    def one_block(args):
        qi, bi = args
        start = bi * BLOCK
        kb = lax.dynamic_slice_in_dim(kp, start, BAND, axis=1)
        vb = lax.dynamic_slice_in_dim(vp, start, BAND, axis=1)
        kpos = start + offs_k
        valid = in_window & ((kpos >= 0) & (kpos < T))[None, :]
        s_band = jnp.where(valid, jnp.einsum('bqhgd,bkhd->bhgqk', qi, kb), MASK_VALUE)
        s_ctx = jnp.einsum('bqhgd,bkhd->bhgqk', qi, kc)
        p = sink_softmax(jnp.concatenate([s_band, s_ctx], axis=-1), sink_hg)
        return jnp.einsum('bhgqk,bkhd->bqhgd', p, jnp.concatenate([vb, vc], axis=1))

    out = lax.map(one_block, (qb, jnp.arange(nb)))
    return out.transpose(1, 0, 2, 3, 4, 5).reshape(B, T, D_ATTN).astype(q.dtype)

def context_gqa(q, k, v, sink):
    B, C = q.shape[0], q.shape[1]
    qf = (q.astype(F32) * HEAD_DIM ** -0.5).reshape(B, C, N_KV_HEADS, GQA_GROUP, HEAD_DIM)
    s = jnp.einsum('bqhgd,bkhd->bhgqk', qf, k.astype(F32))
    p = sink_softmax(s, sink.astype(F32).reshape(N_KV_HEADS, GQA_GROUP))
    return jnp.einsum('bhgqk,bkhd->bqhgd', p, v.astype(F32)).reshape(B, C, D_ATTN).astype(q.dtype)

def token_shift(h, mu_prev, mu_next):
    prev = jnp.pad(h, ((0, 0), (1, 0), (0, 0)))[:, :-1]
    nxt = jnp.pad(h, ((0, 0), (0, 1), (0, 0)))[:, 1:]
    return h + mu_prev * (prev - h) + mu_next * (nxt - h)

def _heads(t):
    return t.reshape(t.shape[0], t.shape[1], N_HEADS_R, RWKV_HEAD)

def rwkv_prepare(z, mu_prev, mu_next, w0, w_up, a0, a_up, k_k, k_a, g_up):
    zs = token_shift(z.astype(F32), mu_prev, mu_next)
    r, k, v, wdf, wdb, adf, adb, gd = _split(zs, RWKV_SPLITS)
    kk = _heads(k * k_k)
    kk = kk * lax.rsqrt(jnp.maximum(jnp.sum(kk * kk, axis=-1, keepdims=True), 1e-12))
    dirs = []
    for d, (wd, ad) in enumerate(((wdf, adf), (wdb, adb))):
        wlog = -jax.nn.softplus(-(w0[d] + jnp.tanh(wd) @ w_up[d])) - 0.5
        decay = jnp.exp(-jnp.exp(wlog))
        a = jax.nn.sigmoid(a0[d] + ad @ a_up[d])
        kd = k * (1 + (a - 1) * k_a)
        dirs.append((_heads(decay), _heads(kd), _heads(a)))
    gate = jax.nn.sigmoid(gd) @ g_up
    return _heads(r), _heads(v), kk, dirs, gate

def wkv_scan(state0, r, w, k, v, kk, a, reverse):
    tm = lambda t: jnp.swapaxes(t, 0, 1)
    xs = (tm(r), tm(w), tm(k), tm(v), tm(-kk), tm(kk * a))

    def step(S, inp):
        r_t, w_t, k_t, v_t, nkk_t, b_t = inp
        sa = jnp.einsum('bhvk,bhk->bhv', S, nkk_t)
        S = S * w_t[:, :, None, :] + sa[..., None] * b_t[:, :, None, :] + v_t[..., None] * k_t[:, :, None, :]
        return S, jnp.einsum('bhvk,bhk->bhv', S, r_t)

    S_final, ys = lax.scan(step, state0, xs, reverse=reverse)
    return S_final, jnp.swapaxes(ys, 0, 1)

def rwkv_output(y, r, v, dirs, gate, r_k, lnx_g, lnx_b):
    B, T = y.shape[0], y.shape[1]
    mean = jnp.mean(y, axis=-1, keepdims=True)
    var = jnp.mean(jnp.square(y - mean), axis=-1, keepdims=True)
    yn = ((y - mean) * lax.rsqrt(var + LNX_EPS)).reshape(B, T, D_RWKV) * lnx_g + lnx_b
    rk = r_k.reshape(N_HEADS_R, RWKV_HEAD)
    bonus = sum(jnp.sum(r * kd * rk, axis=-1, keepdims=True) * v for _, kd, _ in dirs)
    return (yn + bonus.reshape(B, T, D_RWKV)) * gate

def hybrid_layer(x, xc, c, c_ctx, row, col, ada_w, ada_b, norm1_g, norm2_g, w_in, attn_sink,
                 ts_prev, ts_next, w0, w_up, a0, a_up, k_k, k_a, r_k, g_up, lnx_g, lnx_b,
                 w_out, ffn_w1, ffn_w3, ffn_w2, update_ctx):
    B, T = x.shape[0], x.shape[1]
    C = xc.shape[1]
    mod = jax.nn.silu(c) @ ada_w + ada_b
    mod_c = jax.nn.silu(c_ctx) @ ada_w + ada_b
    sh1, sc1, g1, sh2, sc2, g2 = jnp.split(mod[:, None, :], 6, axis=-1)
    sh1c, sc1c, g1c, sh2c, sc2c, g2c = jnp.split(mod_c, 6, axis=-1)

    z = modulate(rmsnorm(x, norm1_g), sh1, sc1) @ w_in
    zc = modulate(rmsnorm(xc, norm1_g), sh1c, sc1c) @ w_in
    za, zr = z[..., :D_IN_ATTN], z[..., D_IN_ATTN:]
    zca, zcr = zc[..., :D_IN_ATTN], zc[..., D_IN_ATTN:]

    q, k, v = _split(za, ATTN_SPLITS)
    q = axial_rope(q.reshape(B, T, N_HEADS_A, HEAD_DIM), row, col)
    k = axial_rope(k.reshape(B, T, N_KV_HEADS, HEAD_DIM), row, col)
    v = v.reshape(B, T, N_KV_HEADS, HEAD_DIM)
    qc, kc, vc = _split(zca, ATTN_SPLITS)
    kc = kc.reshape(B, C, N_KV_HEADS, HEAD_DIM)
    vc = vc.reshape(B, C, N_KV_HEADS, HEAD_DIM)
    attn = windowed_gqa(q, k, v, kc, vc, attn_sink)

    rw_args = (ts_prev, ts_next, w0, w_up, a0, a_up, k_k, k_a, g_up)
    r, vr, kk, dirs, gate = rwkv_prepare(zr, *rw_args)
    rc, vrc, kkc, dirsc, gatec = rwkv_prepare(zcr, *rw_args)
    S0 = jnp.zeros((B, N_HEADS_R, RWKV_HEAD, RWKV_HEAD), F32)
    y_lat = jnp.zeros_like(r)
    yc_dirs = []
    for d in range(2):
        rev = d == 1
        wd, kd, ad = dirs[d]
        wdc, kdc, adc = dirsc[d]
        Sc, yc_d = wkv_scan(S0, rc, wdc, kdc, vrc, kkc, adc, rev)
        _, y_d = wkv_scan(Sc, r, wd, kd, vr, kk, ad, rev)
        y_lat = y_lat + y_d
        yc_dirs.append(yc_d)
    rw = rwkv_output(y_lat, r, vr, dirs, gate, r_k, lnx_g, lnx_b).astype(x.dtype)

    x = x + g1 * (jnp.concatenate([attn, rw], axis=-1) @ w_out)
    x = x + g2 * swiglu(modulate(rmsnorm(x, norm2_g), sh2, sc2), ffn_w1, ffn_w3, ffn_w2)

    if update_ctx:
        attn_c = context_gqa(qc.reshape(B, C, N_HEADS_A, HEAD_DIM), kc, vc, attn_sink)
        rw_c = rwkv_output(yc_dirs[0] + yc_dirs[1], rc, vrc, dirsc, gatec, r_k, lnx_g, lnx_b).astype(xc.dtype)
        xc = xc + g1c * (jnp.concatenate([attn_c, rw_c], axis=-1) @ w_out)
        xc = xc + g2c * swiglu(modulate(rmsnorm(xc, norm2_g), sh2c, sc2c), ffn_w1, ffn_w3, ffn_w2)
    return x, xc

def first_inputs(seed: int = 0) -> dict:
    key = jax.random.key(seed)
    ks = jax.random.split(key, 27)
    nrm = lambda k, shape, s: jax.random.normal(k, shape, jnp.float32) * s
    uni = lambda k, shape, lo, hi: jax.random.uniform(k, shape, jnp.float32, lo, hi)
    L = DEPTH
    return {
        'x': nrm(ks[0], (BATCH, SEQ, D_MODEL), 1.0),
        'c': nrm(ks[1], (BATCH, D_MODEL), 1.0),
        'ctx': nrm(ks[2], (BATCH, CTX_LEN, D_MODEL), 1.0),
        'c_ctx': nrm(ks[3], (D_MODEL,), 1.0),
        'ada_w': nrm(ks[4], (L, D_MODEL, 6 * D_MODEL), 0.5 * D_MODEL ** -0.5),
        'ada_b': nrm(ks[5], (L, 6 * D_MODEL), 0.02),
        'norm1_g': 1.0 + nrm(ks[6], (L, D_MODEL), 0.05),
        'norm2_g': 1.0 + nrm(ks[7], (L, D_MODEL), 0.05),
        'w_in': nrm(ks[8], (L, D_MODEL, D_IN), D_MODEL ** -0.5),
        'attn_sink': nrm(ks[9], (L, N_HEADS_A), 0.5),
        'ts_prev': uni(ks[10], (L, D_IN_RWKV), 0.0, 0.5),
        'ts_next': uni(ks[11], (L, D_IN_RWKV), 0.0, 0.5),
        'w0': uni(ks[12], (L, 2, D_RWKV), -4.0, 1.0),
        'w_up': nrm(ks[13], (L, 2, D_DECAY_LORA, D_RWKV), 0.1),
        'a0': nrm(ks[14], (L, 2, D_RWKV), 0.5),
        'a_up': nrm(ks[15], (L, 2, D_AAA_LORA, D_RWKV), 0.1),
        'k_k': 0.85 + nrm(ks[16], (L, D_RWKV), 0.05),
        'k_a': 1.0 + nrm(ks[17], (L, D_RWKV), 0.05),
        'r_k': nrm(ks[18], (L, D_RWKV), 0.1),
        'g_up': nrm(ks[19], (L, D_GATE_LORA, D_RWKV), D_GATE_LORA ** -0.5),
        'lnx_g': 1.0 + nrm(ks[20], (L, D_RWKV), 0.05),
        'lnx_b': nrm(ks[21], (L, D_RWKV), 0.02),
        'w_out': nrm(ks[22], (L, D_MIX, D_MODEL), D_MIX ** -0.5),
        'ffn_w1': nrm(ks[23], (L, D_MODEL, D_FF), D_MODEL ** -0.5),
        'ffn_w3': nrm(ks[24], (L, D_MODEL, D_FF), D_MODEL ** -0.5),
        'ffn_w2': nrm(ks[25], (L, D_FF, D_MODEL), D_FF ** -0.5),
        'final_norm_g': 1.0 + nrm(ks[26], (D_MODEL,), 0.05),
    }

def first_block(x, c, ctx, c_ctx, ada_w, ada_b, norm1_g, norm2_g, w_in, attn_sink, ts_prev, ts_next,
              w0, w_up, a0, a_up, k_k, k_a, r_k, g_up, lnx_g, lnx_b, w_out, ffn_w1, ffn_w3, ffn_w2,
              final_norm_g):
    seq_len = x.shape[1]
    rows = seq_len // GRID_W
    row = jnp.repeat(jnp.arange(rows, dtype=jnp.int32), GRID_W)
    col = jnp.tile(jnp.arange(GRID_W, dtype=jnp.int32), rows)
    xc = ctx
    for i in range(DEPTH):
        x, xc = hybrid_layer(x, xc, c, c_ctx, row, col, ada_w[i], ada_b[i], norm1_g[i], norm2_g[i],
                             w_in[i], attn_sink[i], ts_prev[i], ts_next[i], w0[i], w_up[i], a0[i],
                             a_up[i], k_k[i], k_a[i], r_k[i], g_up[i], lnx_g[i], lnx_b[i], w_out[i],
                             ffn_w1[i], ffn_w3[i], ffn_w2[i], update_ctx=(i < DEPTH - 1))
    return rmsnorm(x, final_norm_g)


DEPTH_2 = 2

N_A = DEPTH_2 // 2
N_B = DEPTH_2 - N_A
MEM_LEN = 256
RET_HEADS = 8
RET_DK = D_MODEL // 16
RET_DV = 2 * RET_DK
RET_CHUNK = 128
RET_THETA_BASE = 10000.0
DIL_CONFIG = ((128, 1), (512, 4), (2048, 16))
DIL_HEADS = 16
DIL_DH = D_MODEL // 16
DIL_BLOCK = 128
MEM_HEADS = 4
MEM_DH = D_MODEL // 8
EPS = 1e-6

RET_QK_W = RET_HEADS * RET_DK
RET_V_W = RET_HEADS * RET_DV
DIL_W = DIL_HEADS * DIL_DH
MEM_W = MEM_HEADS * MEM_DH
MIX_W_A = RET_V_W + MEM_W
MIX_W_B = DIL_W + MEM_W
IN_W_A = 2 * RET_QK_W + 2 * RET_V_W + 2 * MEM_W
IN_W_B = len(DIL_CONFIG) * DIL_W + DIL_W + 2 * MEM_W
KV_W = 2 * len(DIL_CONFIG) * DIL_W


def split_cols(a, widths):
    idx, acc = [], 0
    for w in widths[:-1]:
        acc += w
        idx.append(acc)
    return jnp.split(a, idx, axis=-1)

def rmsnorm_2(x, g):
    xf = x.astype(jnp.float32)
    y = xf * lax.rsqrt(jnp.mean(xf * xf, axis=-1, keepdims=True) + EPS) * g.astype(jnp.float32)
    return y.astype(x.dtype)

def rotary(t):
    S, half = t.shape[1], t.shape[-1] // 2
    inv = 1.0 / (RET_THETA_BASE ** jnp.linspace(0.0, 1.0, half, dtype=jnp.float32))
    ang = jnp.arange(S, dtype=jnp.float32)[:, None] * inv[None, :]
    cos = jnp.cos(ang)[None, :, None, :]
    sin = jnp.sin(ang)[None, :, None, :]
    tf = t.astype(jnp.float32)
    t1, t2 = tf[..., :half], tf[..., half:]
    return jnp.concatenate([t1 * cos - t2 * sin, t1 * sin + t2 * cos], axis=-1)

def retention(q, k, v):
    B, S, H, Dk = q.shape
    Dv = v.shape[-1]
    C = math.gcd(S, RET_CHUNK)
    N = S // C
    log_g = jnp.log1p(-(2.0 ** (-5.0 - jnp.arange(H, dtype=jnp.float32))))
    qc = q.reshape(B, N, C, H, Dk)
    kc = k.reshape(B, N, C, H, Dk)
    vc = v.astype(jnp.float32).reshape(B, N, C, H, Dv)
    pos = jnp.arange(C, dtype=jnp.float32)
    rel = pos[:, None] - pos[None, :]
    decay_in = jnp.where(rel >= 0, jnp.exp(jnp.maximum(rel, 0.0)[None] * log_g[:, None, None]), 0.0)
    xi = jnp.exp((pos[None, :] + 1.0) * log_g[:, None])
    zeta = jnp.exp((C - 1.0 - pos[None, :]) * log_g[:, None])
    g_chunk = jnp.exp(C * log_g)
    s = jnp.einsum('bnqhd,bnkhd->bnhqk', qc, kc) * decay_in[None, None]
    o_in = jnp.einsum('bnhqk,bnkhe->bnqhe', s, vc)
    U = jnp.einsum('bnkhd,hk,bnkhe->bnhde', kc, zeta, vc)

    def step(R, U_n):
        return g_chunk[None, :, None, None] * R + U_n, R

    _, R_prev = lax.scan(step, jnp.zeros_like(U[:, 0]), jnp.moveaxis(U, 1, 0))
    cross = jnp.einsum('bnqhd,nbhde->bnqhe', qc, R_prev) * xi.T[None, None, :, :, None]
    return (o_in + cross).reshape(B, S, H, Dv)

def memory_branch(mq, gate, mem_n, w_mem_kv):
    B, S, _ = mq.shape
    M = mem_n.shape[1]
    mk, mv = split_cols(mem_n @ w_mem_kv, [MEM_W, MEM_W])
    q = mq.reshape(B, S, MEM_HEADS, MEM_DH)
    k = mk.reshape(B, M, MEM_HEADS, MEM_DH)
    v = mv.reshape(B, M, MEM_HEADS, MEM_DH)
    s = jnp.einsum('bshd,bmhd->bhsm', q, k).astype(jnp.float32) * (MEM_DH ** -0.5)
    p = jax.nn.softmax(s, axis=-1)
    o = jnp.einsum('bhsm,bmhd->bshd', p.astype(v.dtype), v).reshape(B, S, MEM_W)
    return o * jax.nn.silu(gate)

def dilated_group(q, k, v, dil, span):
    B, S, H, D = q.shape
    n = S // dil
    Qb = math.gcd(n, DIL_BLOCK)
    nb = n // Qb

    def to_res(t):
        return t.reshape(B, n, dil, H, D).transpose(0, 2, 1, 3, 4)

    qr = to_res(q).reshape(B, dil, nb, Qb, H, D)
    pad = ((0, 0), (0, 0), (span, 0), (0, 0), (0, 0))
    kr = jnp.pad(to_res(k), pad)
    vr = jnp.pad(to_res(v), pad)
    idx = jnp.arange(nb)[:, None] * Qb + jnp.arange(Qb + span)[None, :]
    kb = kr[:, :, idx]
    vb = vr[:, :, idx]
    dist = jnp.arange(Qb)[:, None] + span - jnp.arange(Qb + span)[None, :]
    band = (dist >= 0) & (dist <= span)
    mask = band[None] & ((idx - span)[:, None, :] >= 0)
    s = jnp.einsum('bgnqhd,bgnkhd->bgnhqk', qr, kb).astype(jnp.float32) * (D ** -0.5)
    s = jnp.where(mask[None, None, :, None], s, -1e30)
    m = jnp.max(s, axis=-1, keepdims=True)
    p = jnp.exp(s - m)
    l = jnp.sum(p, axis=-1)
    o = jnp.einsum('bgnhqk,bgnkhd->bgnqhd', p, vb.astype(jnp.float32))
    o = o / jnp.transpose(l, (0, 1, 2, 4, 3))[..., None]
    lse = jnp.transpose(m[..., 0] + jnp.log(l), (0, 1, 2, 4, 3))
    o = o.reshape(B, dil, n, H, D).transpose(0, 2, 1, 3, 4).reshape(B, S, H, D)
    lse = lse.reshape(B, dil, n, H).transpose(0, 2, 1, 3).reshape(B, S, H)
    return o, lse

def retention_layer(x, g, w_in, w_mem_kv, w_out, mem_n):
    B, S, _ = x.shape
    h = rmsnorm_2(x, g)
    q, k, v, gate_r, mq, gate_m = split_cols(h @ w_in, [RET_QK_W, RET_QK_W, RET_V_W, RET_V_W, MEM_W, MEM_W])
    q = rotary(q.reshape(B, S, RET_HEADS, RET_DK))
    k = rotary(k.reshape(B, S, RET_HEADS, RET_DK)) * (RET_DK ** -0.5)
    o = retention(q, k, v.reshape(B, S, RET_HEADS, RET_DV))
    o = o * lax.rsqrt(jnp.mean(o * o, axis=-1, keepdims=True) + EPS)
    o_ret = o.reshape(B, S, RET_V_W).astype(x.dtype) * jax.nn.silu(gate_r)
    o_mem = memory_branch(mq, gate_m, mem_n, w_mem_kv)
    return x + jnp.concatenate([o_ret, o_mem], axis=-1) @ w_out

def shared_kv(x, g, w_kv):
    B, S, _ = x.shape
    parts = split_cols(rmsnorm_2(x, g) @ w_kv, [DIL_W] * (2 * len(DIL_CONFIG)))
    return [t.reshape(B, S, DIL_HEADS, DIL_DH) for t in parts]

def dilated_layer(x, g, w_in, w_mem_kv, w_out, mem_n, kv):
    B, S, _ = x.shape
    h = rmsnorm_2(x, g)
    n_g = len(DIL_CONFIG)
    parts = split_cols(h @ w_in, [DIL_W] * n_g + [DIL_W, MEM_W, MEM_W])
    gate_d, mq, gate_m = parts[n_g], parts[n_g + 1], parts[n_g + 2]
    outs, lses = [], []
    for gi, (window, dil) in enumerate(DIL_CONFIG):
        q = parts[gi].reshape(B, S, DIL_HEADS, DIL_DH)
        o, lse = dilated_group(q, kv[2 * gi], kv[2 * gi + 1], dil, window // dil)
        outs.append(o)
        lses.append(lse)
    alpha = jax.nn.softmax(jnp.stack(lses, axis=0), axis=0)
    o = jnp.sum(alpha[..., None] * jnp.stack(outs, axis=0), axis=0)
    o_dil = o.reshape(B, S, DIL_W).astype(x.dtype) * jax.nn.silu(gate_d)
    o_mem = memory_branch(mq, gate_m, mem_n, w_mem_kv)
    return x + jnp.concatenate([o_dil, o_mem], axis=-1) @ w_out

def second_inputs(seed: int = 0) -> dict:
    key = jax.random.key(seed)
    ks = jax.random.split(key, 14)
    f32 = jnp.float32

    def w(k, shape, fan_in):
        return jax.random.normal(k, shape, f32) * (fan_in ** -0.5)

    def gain(k, shape):
        return 1.0 + 0.02 * jax.random.normal(k, shape, f32)

    return {
        "x": jax.random.normal(ks[0], (BATCH, SEQ, D_MODEL), f32),
        "mem": jax.random.normal(ks[1], (BATCH, MEM_LEN, D_MODEL), f32),
        "norm_a": gain(ks[2], (N_A, D_MODEL)),
        "w_in_a": w(ks[3], (N_A, D_MODEL, IN_W_A), D_MODEL),
        "w_out_a": w(ks[4], (N_A, MIX_W_A, D_MODEL), MIX_W_A),
        "norm_b": gain(ks[5], (N_B, D_MODEL)),
        "w_in_b": w(ks[6], (N_B, D_MODEL, IN_W_B), D_MODEL),
        "w_out_b": w(ks[7], (N_B, MIX_W_B, D_MODEL), MIX_W_B),
        "w_mem_kv": w(ks[8], (DEPTH_2, D_MODEL, 2 * MEM_W), D_MODEL),
        "mem_norm_g": gain(ks[9], (D_MODEL,)),
        "kv_norm_g": gain(ks[10], (D_MODEL,)),
        "w_kv": w(ks[11], (D_MODEL, KV_W), D_MODEL),
        "final_norm_g": gain(ks[12], (D_MODEL,)),
    }

def second_block(x, mem, norm_a, w_in_a, w_out_a, norm_b, w_in_b, w_out_b, w_mem_kv, mem_norm_g, kv_norm_g, w_kv, final_norm_g):
    mem_n = rmsnorm_2(mem, mem_norm_g)
    kv = None
    for layer in range(DEPTH_2):
        if layer < N_A:
            x = retention_layer(x, norm_a[layer], w_in_a[layer], w_mem_kv[layer], w_out_a[layer], mem_n)
            if layer == N_A - 1:
                kv = shared_kv(x, kv_norm_g, w_kv)
        else:
            j = layer - N_A
            x = dilated_layer(x, norm_b[j], w_in_b[j], w_mem_kv[layer], w_out_b[j], mem_n, kv)
    return rmsnorm_2(x, final_norm_g)


def setup_inputs(seed=0):
    out = dict(first_inputs(seed))
    for name, value in second_inputs(seed + 1).items():
        if name != "x":
            out[name + "_2"] = value
    return out


def reference(
    x, c, ctx, c_ctx, ada_w, ada_b, norm1_g, norm2_g, w_in, attn_sink, ts_prev, ts_next, w0,
    w_up, a0, a_up, k_k, k_a, r_k, g_up, lnx_g, lnx_b, w_out, ffn_w1, ffn_w3, ffn_w2,
    final_norm_g, mem_2, norm_a_2, w_in_a_2, w_out_a_2, norm_b_2, w_in_b_2, w_out_b_2,
    w_mem_kv_2, mem_norm_g_2, kv_norm_g_2, w_kv_2, final_norm_g_2,
):
    x = first_block(
        x, c, ctx, c_ctx, ada_w, ada_b, norm1_g, norm2_g, w_in, attn_sink, ts_prev, ts_next, w0,
        w_up, a0, a_up, k_k, k_a, r_k, g_up, lnx_g, lnx_b, w_out, ffn_w1, ffn_w3, ffn_w2,
        final_norm_g,
    )
    return second_block(
        x, mem_2, norm_a_2, w_in_a_2, w_out_a_2, norm_b_2, w_in_b_2, w_out_b_2, w_mem_kv_2,
        mem_norm_g_2, kv_norm_g_2, w_kv_2, final_norm_g_2,
    )


_drawn_inputs = setup_inputs


def setup_inputs(seed=0):
    import zlib

    import numpy as np

    out = dict(_drawn_inputs(seed))
    spreads = {}
    factors = {'attn_sink': 8.0,
     'k_a': 4.019,
     'lnx_g': 7.203,
     'lnx_b': 8.0,
     'norm_b_2': 8.0,
     'mem_norm_g_2': 8.0,
     'kv_norm_g_2': 8.0,
     'final_norm_g_2': 2.727}
    for name, (base, spread) in spreads.items():
        noise = np.random.default_rng([zlib.crc32(name.encode()), seed]).standard_normal(out[name].shape)
        drawn = base * np.exp(spread * noise) if base else spread * noise
        out[name] = jnp.asarray(drawn.astype(out[name].dtype))
    for name, factor in factors.items():
        out[name] = (out[name] * factor).astype(out[name].dtype)
    return out
```

```python
from contextlib import ExitStack

import numpy as np

import concourse.bass as bass
from concourse import mybir

F32 = mybir.dt.float32
F32R = mybir.dt.float32r
ALU = mybir.AluOpType
ACT = mybir.ActivationFunctionType
AX = mybir.AxisListType
MUL, ADD, SUB, MAX, BYP = ALU.mult, ALU.add, ALU.subtract, ALU.max, ALU.bypass

T = 256
NRAW = 6
NW = 4
AHEAD = 3
NG = 4
NX = 4
NEG = -1e30
DECAY = float(np.exp(-0.5))


def do(method, *args, **kw):
    return lambda: method(*args, **kw)


class Count:

    def __init__(self, sem):
        self.sem, self.n = sem, 0

    def add(self, by):
        self.n += by
        return (self, self.n)


class Engine:

    def __init__(self, nc, sem):
        self.nc, self.count, self.queue, self.seen = nc, Count(sem), [], {}

    def waits(self, deps):
        need = {}
        for d in flat(deps):
            if d[1] > max(self.seen.get(d[0], 0), need.get(d[0], 0)):
                need[d[0]] = d[1]
        self.seen.update(need)
        return [(c.sem, v) for c, v in need.items()]

    def __call__(self, fn, *deps, inc=True):
        token = self.count.add(1) if inc else None
        self.queue.append((self.waits(deps), fn, self.count.sem if inc else None, 1))
        return token

    def dma(self, out, in_, count, *deps):
        token = count.add(16)
        self.queue.append((self.waits(deps), do(self.nc.dma_start, out, in_), count.sem, 16))
        return token

    def last(self):
        return (self.count, self.count.n) if self.count.n else None

    def emit(self, e):
        for waits, fn, sem, by in self.queue:
            for s, v in waits:
                e.wait_ge(s, v)
            if fn is not None:
                ins = fn()
                if sem is not None:
                    ins.then_inc(sem, by)


def flat(deps):
    for d in deps:
        if isinstance(d, list):
            yield from flat(d)
        elif d is not None:
            yield d


class Pool:

    def __init__(self, views):
        self.views, self.free = views, [(i, []) for i in range(len(views))]

    def get(self):
        i, deps = self.free.pop(0)
        return Buf(self, i, self.views[i], deps)


class Buf:
    def __init__(self, pool, i, ap, deps):
        self.pool, self.i, self.ap, self.deps, self.tok = pool, i, ap, deps, []

    def done(self, *tokens):
        self.pool.free.append((self.i, list(flat(tokens))))


class Acts:

    def __init__(self, hi, lo):
        self.hi, self.lo = hi, lo
        self.tok = [[] for _ in range(hi.shape[1])]


def run_all(*gens):
    live = list(gens)
    while live:
        for g in list(live):
            for _ in range(g[1]):
                if next(g[0], "end") == "end":
                    live.remove(g)
                    break


def rest(g):
    for _ in g:
        pass


def build(nc, io, out, sems, mem, order):
    SP, PE, DVE, AC, PO = (Engine(e, sems[f"e{i}"]) for i, e in enumerate((nc.sync, nc.tensor, nc.vector, nc.scalar, nc.gpsimd)))
    engines = (SP, PE, DVE, AC, PO)
    new_sem = iter(range(100))

    def counter():
        return Count(sems[f"d{next(new_sem)}"])

    def fence():
        return [e.last() for e in engines]

    A = mem.__getitem__
    ps = A("ps")

    raw_sem = [counter() for _ in range(NRAW)]
    rec = []
    slots = {}
    gate = dict(at=0 if order is None else next(i for i, k in enumerate(order) if k[0] == "w_out"), deps=[])
    st = dict(i=0, split=0, dma=0, nsplit=0)
    released = {}
    wdone = {}

    def emit_dma(j):
        name, nt, kg, w, split = order[j]
        src = io[name][nt, kg] if split != "tail" else io[name][kg]
        dst = A("raw")[:, j % NRAW, 0:4 * w]
        slots[j] = dict(raw=dst.rearrange("p (c n) -> p c n", c=4), w=w,
                        tok=SP.dma(dst, src.rearrange("p c n -> p (c n)"), raw_sem[j % NRAW],
                                   released.get(j - NRAW)))
        st["dma"] += 1

    def emit_split(j):
        s = slots[j]
        w = s["w"]
        if order[j][4] == "raw":
            return
        n = st["nsplit"]
        st["nsplit"] += 1
        s["n"] = n
        src = A("raw")[:, j % NRAW, 0:4 * w]
        hi, lo = A("wh")[:, n % NW, 0:4 * w], A("wl")[:, n % NW, 0:4 * w]
        t1 = AC(do(nc.scalar.activation, hi, src, ACT.Copy), s["tok"], wdone.get(n - NW), gate["deps"])
        eng = DVE if n % 2 else PO
        t2 = eng(do(eng.nc.tensor_tensor, lo, src, hi.bitcast(F32), SUB), s["tok"], t1, wdone.get(n - NW), gate["deps"])
        s["hi"], s["lo"] = (v.rearrange("p (c n) -> p c n", c=4) for v in (hi, lo))
        s["ready"] = [t1, t2]
        released[j] = [t1, t2]

    def next_slot(key):
        i = st["i"]
        st["i"] += 1
        if order is None:
            rec.append(key)
            w = key[3]
            hi = A("wh")[:, 0, 0:4 * w].rearrange("p (c n) -> p c n", c=4)
            return i, dict(raw=A("raw")[:, 0, 0:4 * w].rearrange("p (c n) -> p c n", c=4), hi=hi, lo=hi,
                           ready=[], tok=None, n=0)
        assert order[i] == key
        for j in range(st["split"], min(i + AHEAD + 1, gate["at"])):
            while st["dma"] <= j:
                emit_dma(st["dma"])
            emit_split(j)
            st["split"] = j + 1
        while st["dma"] < len(order) and (st["dma"] < NRAW or st["dma"] - NRAW in released):
            emit_dma(st["dma"])
        return i, slots[i]

    def open_gate(deps):
        if order is not None:
            gate.update(at=len(order), deps=deps)

    def slot_done(i, s, token):
        if order is None:
            return
        if order[i][4] == "raw":
            released[i] = [token]
        else:
            wdone[s["n"]] = token

    G = Pool([ps[:, b, :] for b in range(NG)])
    X = Pool([ps[:, NG + b, :] for b in range(NX)])

    def two(pool):
        ids = {i: k for k, (i, _) in enumerate(pool.free)}
        for i in (0, 2):
            if i in ids and i + 1 in ids:
                parts = [f for f in pool.free if f[0] in (i, i + 1)]
                pool.free = [f for f in pool.free if f[0] not in (i, i + 1)]
                return Two(pool, i, [d for _, d in parts])
        raise RuntimeError("no two banks")

    class Two:
        def __init__(self, pool, i, deps):
            self.pool, self.i, self.deps = pool, i, deps
            base = NG + i if pool is X else i
            self.ap = ps[:, base:base + 2, :].rearrange("p b n -> p (b n)")

        def done(self, *tokens):
            for k in (self.i, self.i + 1):
                self.pool.free.append((k, list(flat(tokens))))

    def gemm(name, nt, kgs, outs, nb, evac, w=256, split=True, deps=None, kbase=0):
        banks = [G.get() for _ in range(nb)]
        begun = set()
        for at, kg in enumerate(kgs):
            i, s = next_slot((name, nt, kg, w, split))
            wait = [s["ready"], deps] if deps else s["ready"]
            hi, lo = s["hi"], s["lo"]
            for kc in range(4):
                k = (kg - kbase) * 4 + kc
                for n, (b, off, kind, c0, acts, tb) in enumerate(outs):
                    ah, al = acts.hi[:, k, :], acts.lo[:, k, :]
                    if kind == "B":
                        o = banks[b].ap[:, off:off + T]
                        pairs = [(hi[:, kc, c0:c0 + 128], ah), (hi[:, kc, c0:c0 + 128], al),
                                 (lo[:, kc, c0:c0 + 128], ah)]
                    else:
                        o = banks[b].ap[:, off:off + w]
                        r = slice(128 * tb, 128 * tb + 128)
                        pairs = [(ah[:, r], hi[:, kc, :]), (ah[:, r], lo[:, kc, :]), (al[:, r], hi[:, kc, :])]
                    for m, (x, y) in enumerate(pairs):
                        first = b not in begun
                        begun.add(b)
                        end = kc == 3 and n == len(outs) - 1 and m == 2
                        last = at == len(kgs) - 1 and kc == 3 and m == 2
                        tok = PE(do(nc.tensor.matmul, o, x, y, start=first, stop=last, skip_group_check=True),
                                 wait, acts.tok[k], banks[b].deps if first else None, inc=end)
                        wait = None
            slot_done(i, s, tok)
            yield
        evac(banks, tok)

    cs = A("const")

    def cst(name, n):
        o = COLS[name]
        return cs[:, o:o + n]

    c_load = counter()
    const_tok = SP.dma(cs[:, 0:NCONST], io["consts"], c_load)
    ident, ones, blk = cst("ident", 128), cst("ones", 128), cst("blk", 128)

    tmps = Pool([A("tm")[:, i, :] for i in range(4)])
    rsts = Pool([A("rst")[:, i, :] for i in range(2)])
    xt = A("x")

    def rms(src, nch, deps, sq, eps=1e-6):
        bank = X.get()
        for q in range(nch // 4):
            b = sq.get()
            t = AC(do(nc.scalar.activation, b.ap, src[:, 4 * q:4 * q + 4, :], ACT.Square), deps, b.deps)
            for c in range(4):
                m = PE(do(nc.tensor.matmul, bank.ap[:, 0:T], ones, b.ap[:, c, :],
                                                         start=(q == 0 and c == 0), stop=(q == nch // 4 - 1 and c == 3)),
                       t, const_tok, bank.deps, inc=(c == 3))
            b.done(m)
        r = rsts.get()
        d1 = DVE(do(nc.vector.tensor_scalar, r.ap, bank.ap[:, 0:T], 1.0 / (128 * nch), eps, MUL, ADD), m, r.deps)
        bank.done(d1)
        d2 = AC(do(nc.scalar.activation, r.ap, r.ap, ACT.Sqrt), d1)
        r.tok = DVE(do(nc.vector.reciprocal, r.ap, r.ap), d2)
        return r

    def split(dst, c, n, src, *deps):
        hi, lo = dst.hi[:, c:c + n, :], dst.lo[:, c:c + n, :]
        t1 = AC(do(nc.scalar.activation, hi, src, ACT.Copy), *deps)
        t2 = PO(do(nc.gpsimd.tensor_tensor, lo, src, hi.bitcast(F32), SUB), t1, *deps)
        for k in range(c, c + n):
            dst.tok[k] = [t1, t2]
        return [t1, t2]

    def normed(src, r, gain, shift, dst, deps):
        for c in range(16):
            b = tmps.get()
            t = DVE(do(nc.vector.scalar_tensor_tensor, b.ap, src[:, c, :], gain[:, c:c + 1], r.ap, MUL, MUL),
                    r.tok, b.deps, deps)
            hi, lo = dst.hi[:, c, :], dst.lo[:, c, :]
            if shift is None:
                b.done(split(dst, c, 1, b.ap.rearrange("p (o n) -> p o n", o=1), t, deps))
            else:
                t1 = AC(do(nc.scalar.activation, hi, b.ap, ACT.Identity, bias=shift[:, c:c + 1]), t, deps)
                t2 = DVE(do(nc.vector.scalar_tensor_tensor, lo, b.ap, shift[:, c:c + 1], hi.bitcast(F32), ADD, SUB), t1)
                dst.tok[c] = [t1, t2]
                b.done(t1, t2)
        r.done(t)

    def tanh_half(dst, src, *deps):
        return AC(do(nc.scalar.activation, dst, src, ACT.Tanh, scale=0.5), *deps)

    HA, HB = Acts(A("hah"), A("hal")), Acts(A("hbh"), A("hbl"))
    mix = A("mix")
    work4 = Pool([A("work")[:, 1024 * i:1024 * i + 1024].rearrange("p (c n) -> p c n", c=4) for i in range(7)])

    m32, l_m, l_c, l_x = A("hal32").rearrange("p (c n) -> p c n", c=16), counter(), counter(), counter()
    m_tok = SP.dma(m32, io["memT"], l_m)
    c_tok = SP.dma(mix[:, 0:16, :], io["ctxT"], l_c)
    x_tok = SP.dma(xt, io["xT"], l_x)
    sc = A("sc")
    th = tmps.get()
    cv = cst("c", 32)
    t = tanh_half(th.ap[:, 0:32], cv, const_tok)
    t = DVE(do(nc.vector.scalar_tensor_tensor, sc, th.ap[:, 0:32], 1.0, cv, ADD, MUL), t)
    sc_tok = DVE(do(nc.vector.tensor_scalar, sc, sc, 0.5, None, MUL), t)
    th.done(sc_tok)
    sc16 = A("sc16")
    sc_tok = DVE(do(nc.vector.tensor_copy, sc16.rearrange("p (k n) -> p k n", n=16), sc.unsqueeze(2).to_broadcast([128, 32, 16])), sc_tok)
    mod = A("mod")
    ada_b, sel = cst("ada_b", 96), cst("sel", 2)
    mod_tok = {}

    def ada(nt):
        bank = G.get()
        for kg in range(4):
            i, s = next_slot(("ada", nt, kg, 256, "raw"))
            for g in range(4):
                k = 4 * kg + g
                w = sc16[:, 32 * k:32 * k + 32]
                tok = PE(do(nc.tensor.matmul, bank.ap[32 * g:32 * g + 32, 0:256], w, s["raw"][:, g, :], start=(kg == 0),
                            stop=(kg == 3), skip_group_check=True),
                         s["tok"], sc_tok, bank.deps if kg == 0 else None, inc=(g == 3))
            slot_done(i, s, tok)
            yield
        part = tmps.get()
        t = AC(do(nc.scalar.activation, part.ap, bank.ap[:, 0:256], ACT.Copy), tok, part.deps)
        yield
        for fb in range(2):
            tok = PE(do(nc.tensor.matmul, bank.ap[:, 256 + 2 * fb:258 + 2 * fb], part.ap[:, 128 * fb:128 * fb + 128], sel,
                        start=True, stop=True, skip_group_check=True), t, const_tok, inc=(fb == 1))
        part.done(tok)
        dst = mod[:, 4 * nt:4 * nt + 4].rearrange("p (f t) -> p f t", t=2)
        src = bank.ap[:, 256:260].rearrange("p (f t) -> p f t", t=2)
        b = ada_b[:, 2 * nt:2 * nt + 2].unsqueeze(2).to_broadcast([128, 2, 2])
        mod_tok[nt] = DVE(do(nc.vector.tensor_tensor, dst, src, b, ADD), tok, const_tok)
        bank.done(mod_tok[nt])

    sq4 = Pool(work4.views[0:4])
    wsp = A("work")
    spill = Pool([wsp[:, 4096 + 512 * i:4608 + 512 * i] for i in range(6)])
    s_mem = [counter() for _ in range(6)]
    mem_saved = {}

    def memory_kv():
        for lay in range(2):
            for n in range(8):
                def ev(banks, tok):
                    b = spill.get()
                    t = AC(do(nc.scalar.activation, b.ap, banks[0].ap, ACT.Copy), tok, b.deps)
                    banks[0].done(t)
                    mem_saved[lay, n] = PO.dma(io["mem_keep"][lay, n], b.ap, s_mem[b.i], t)
                    b.done(mem_saved[lay, n])
                outs = [(0, 256 * i, "B", 128 * i, HB, 0) if n < 4 else (0, 256 * i, "A", 0, HB, i) for i in range(2)]
                yield from gemm(f"mem{lay}", n, range(4), outs, 1, ev)

    rm = rms(m32, 16, m_tok, sq4)
    normed(m32, rm, cst("mem_g", 16), None, HB, [const_tok])
    rc = rms(mix, 16, c_tok, sq4)
    rx = rms(xt, 16, x_tok, sq4)

    def ada_first():
        for nt in range(16):
            yield from ada(nt)

    run_all((ada_first(), 1), (memory_kv(), 1))
    f_mem = fence()
    mods = mod.rearrange("p (s c t) -> p s t c", s=6, t=2)

    def plus_one(dst, gain, scale, *deps):
        return DVE(do(nc.vector.scalar_tensor_tensor, dst, scale, 1.0, gain, ADD, MUL), *deps)

    gs = A("gs")
    g1x = plus_one(gs[:, 0:16], cst("norm1", 16), mods[:, 1, 0, :], mod_tok[15], const_tok)
    g1c = plus_one(gs[:, 16:32], cst("norm1", 16), mods[:, 1, 1, :], mod_tok[15], const_tok)
    normed(mix, rc, gs[:, 16:32], mods[:, 0, 1, :], HB, [g1c, mod_tok[7], f_mem])
    normed(xt, rx, gs[:, 0:16], mods[:, 0, 0, :], HA, [g1x, mod_tok[7], f_mem])

    ph = counter()
    phc = A("phc")
    cosr, sinr, amask = phc[:, 0:256], phc[:, 256:512], phc[:, 512:1024].rearrange("p (q n) -> p q n", q=2)
    ph_tok = SP.dma(phc[:, 0:1024], io["attn_c"], ph)
    wk = A("work")
    vT = wk[:, 0:4096].rearrange("p (c n) -> p c n", c=8)
    kA = wk[:, 4096:5120].rearrange("p (c n) -> p c n", c=2)
    vA = wk[:, 5120:6144].rearrange("p (b n) -> p b n", b=4)
    wdad = wk[:, 6144:7168].rearrange("p (c n) -> p c n", c=2)
    gd = wk[:, 7168:7680].rearrange("p (c n) -> p c n", c=2)
    kT = A("xk")
    qT, rT = A("hb_q"), A("hb_r")
    after_norm = [fence(), list(mem_saved.values())]
    ts = cst("ts", 56)
    ts_rem = A("tsr")
    t = DVE(do(nc.vector.tensor_tensor, ts_rem, ts[:, 0:28], ts[:, 28:56], ADD), const_tok)
    tsr_tok = DVE(do(nc.vector.tensor_scalar, ts_rem, ts_rem, -1.0, 1.0, MUL, ADD), t)

    def shift_self(dst, src, f, *deps):
        return AC(do(nc.scalar.activation, dst, src, ACT.Copy, scale=ts_rem[:, f:f + 1]), tsr_tok, *deps)

    def shifted(dst, src, f, nseq, t):
        d3, s3 = (v.rearrange("p (q n) -> p q n", q=nseq) for v in (dst, src))
        t = DVE(do(nc.vector.scalar_tensor_tensor, d3[:, :, 1:T], s3[:, :, 0:T - 1], ts[:, f:f + 1], d3[:, :, 1:T],
                                                 MUL, ADD), t)
        return DVE(do(nc.vector.scalar_tensor_tensor, d3[:, :, 0:T - 1], s3[:, :, 1:T], ts[:, 28 + f:29 + f],
                                                    d3[:, :, 0:T - 1], MUL, ADD), t)

    both = [(fb, 256 * a, "B", 128 * fb, (HB, HA)[a], 0) for fb in range(2) for a in range(2)]
    xonly = [(0, 256 * fb, "B", 128 * fb, HA, 0) for fb in range(2)]
    ztok = {}
    dead = [after_norm]

    def ev_shift2(dst, f0, key):
        def ev(banks, tok):
            for fb in range(2):
                t = shift_self(dst(fb), banks[fb].ap, f0 + fb, tok, dead)
                t = shifted(dst(fb), banks[fb].ap, f0 + fb, 2, t)
                banks[fb].done(t)
                ztok[key, fb] = t
        return ev

    for n in range(4):
        rest(gemm("w_k", n, range(4), both, 2, ev_shift2(lambda fb, n=n: kT[:, 2 * n + fb, :], 8 + 2 * n, ("k", n))))
    for n in range(4):
        rest(gemm("w_v", n, range(4), both, 2, ev_shift2(lambda fb, n=n: vT[:, 2 * n + fb, :], 16 + 2 * n, ("v", n))))
    rest(gemm("w_wa", 0, range(4), both, 2, ev_shift2(lambda fb: wdad[:, fb, :], 24, "wa")))

    def rope(dst, bank, off, w, scale, tok, rot, cos, sin, ctok):
        raw = tmps.get()
        t1 = AC(do(nc.scalar.activation, raw.ap, bank.ap[:, off:off + w], ACT.Copy, scale=scale), tok, raw.deps)
        b = X.get()
        t2 = PE(do(nc.tensor.matmul, b.ap[:, 0:w], rot, raw.ap, start=True, stop=True), t1, const_tok, b.deps)
        t3 = PO(do(nc.gpsimd.tensor_tensor, dst, raw.ap, cos, MUL), t1, ctok, dead)
        t4 = DVE(do(nc.vector.tensor_tensor, raw.ap, b.ap[:, 0:w], sin, MUL), t2, t3, ctok)
        b.done(t4)
        t5 = DVE(do(nc.vector.tensor_tensor, dst, dst, raw.ap, ADD), t4)
        raw.done(t5)
        return t1, t5

    def ev_kA(banks, tok):
        for fb in range(2):
            t0 = AC(do(nc.scalar.activation, kA[:, fb, 256:512], banks[fb].ap[:, 0:256], ACT.Copy), tok, dead)
            t1, t2 = rope(kA[:, fb, 0:256], banks[fb], 256, 256, 1.0, tok, cst("rot32", 128), cosr, sinr, ph_tok)
            banks[fb].done(t0, t1)
            ztok["kA", fb] = [t0, t2]

    rest(gemm("w_ka", 0, range(4), both, 2, ev_kA))

    def ev_vA(banks, tok):
        for b in range(2):
            t = AC(do(nc.scalar.activation, vA[:, 2 * b:2 * b + 2, :], banks[b].ap.rearrange("p (o n) -> p o n", o=2),
                                               ACT.Copy), tok, dead)
            banks[b].done(t)
            ztok["vA", b] = t

    rest(gemm("w_va", 0, range(4), [(a, 256 * tb, "A", 0, (HA, HB)[a], tb) for a in range(2) for tb in range(2)], 2, ev_vA))
    hb_free = fence()

    def ev_r(n):
        def ev(banks, tok):
            own = [shift_self(rT[:, 2 * n + fb, :], banks[0].ap[:, 256 * fb:256 * fb + 256], 2 * n + fb, tok, hb_free)
                   for fb in range(2)]
            for fb in range(2):
                t = shifted(rT[:, 2 * n + fb, :], banks[0].ap[:, 256 * fb:256 * fb + 256], 2 * n + fb, 1, own)
                ztok["r", 2 * n + fb] = t
            banks[0].done(t)
        return ev

    def ev_q(n):
        def ev(banks, tok):
            dead.append(hb_free)
            ts_ = []
            for fb in range(2):
                t1, t2 = rope(qT[:, 2 * n + fb, :], banks[0], 256 * fb, 256, 0.125, tok, cst("rot32", 128), cosr, sinr, ph_tok)
                ts_.append(t1)
                ztok["q", 2 * n + fb] = t2
            banks[0].done(ts_)
        return ev

    def ev_gd(banks, tok):
        own = [shift_self(gd[:, fb, :], banks[0].ap[:, 256 * fb:256 * fb + 256], 26 + fb, tok, dead) for fb in range(2)]
        out_ = []
        for fb in range(2):
            t = shifted(gd[:, fb, :], banks[0].ap[:, 256 * fb:256 * fb + 256], 26 + fb, 1, own)
            out_.append(t)
            t = tanh_half(gd[:, fb, :], gd[:, fb, :], t)
            ztok["gd", fb] = DVE(do(nc.vector.tensor_scalar, gd[:, fb, :], gd[:, fb, :], 0.5, 0.5, MUL, ADD), t)
        banks[0].done(out_)

    for n in range(4):
        rest(gemm("w_q", n, range(4), xonly, 1, ev_q(n)))

    al = A("hbl32")
    pbuf = Pool([al[:, 512 * i:512 * i + 512] for i in range(3)])
    ptbuf = Pool([al[:, 1536 + 512 * i:2048 + 512 * i].rearrange("p (b n) -> p b n", b=4) for i in range(3)])
    cols = A("cols")
    sink = cst("sink", 16)

    def attn():
        out_bank = {}

        def soft(n):
            c, rem = divmod(n, 4)
            half, qb = divmod(rem, 2)
            r = slice(64 * half, 64 * half + 64)
            b = X.get()
            t = PE(do(nc.tensor.matmul, b.ap, qT[r, c, 128 * qb:128 * qb + 128], kA[r, c // 4, :], start=True, stop=True),
                   ztok["q", c], ztok["kA", c // 4], b.deps)
            p = pbuf.get()
            k = 8 * (n % 8)
            mx, nm, rs, es = (cols[:, k + i:k + i + 1] for i in range(4))
            sk = sink[:, 2 * c + half:2 * c + half + 1]
            t0 = AC(do(nc.scalar.activation, p.ap[:, 256:512], b.ap[:, 256:512], ACT.Copy), t, p.deps, hb_free)
            t1 = DVE(do(nc.vector.tensor_tensor, p.ap[:, 0:256], b.ap[:, 0:256], amask[:, qb, :], ADD), t0, p.deps, ph_tok, hb_free)
            b.done(t0, t1)
            t2 = DVE(do(nc.vector.tensor_reduce, mx, p.ap, AX.X, MAX), t0, t1)
            t3 = DVE(do(nc.vector.tensor_scalar, nm, mx, sk, -1.0, MAX, MUL), t2)
            t4 = AC(do(nc.scalar.activation, p.ap, p.ap, ACT.Exp, bias=nm, accum_out=rs), t3)
            t5 = AC(do(nc.scalar.activation, es, sk, ACT.Exp, bias=nm), t3)
            t6 = DVE(do(nc.vector.tensor_tensor, rs, rs, es, ADD), t4, t5)
            t7 = DVE(do(nc.vector.reciprocal, rs, rs), t6)
            p.tok = DVE(do(nc.vector.tensor_scalar, p.ap, p.ap, rs, None, MUL), t7)
            return p

        def apply(n, p):
            c, rem = divmod(n, 4)
            half, qb = divmod(rem, 2)
            kv = 2 * (c // 4) + half
            b = X.get()
            for k in range(4):
                t = PE(do(nc.tensor.transpose, b.ap[:, 128 * k:128 * k + 128], p.ap[:, 128 * k:128 * k + 128], ident),
                       p.tok, b.deps, inc=(k == 3))
            p.done(t)
            pt = ptbuf.get()
            t1 = AC(do(nc.scalar.activation, pt.ap, b.ap.rearrange("p (b n) -> p b n", b=4), ACT.Copy), t, pt.deps, hb_free)
            b.done(t1)
            yield
            if rem == 0:
                out_bank[c] = X.get()
            o = out_bank[c]
            for k in range(4):
                t = PE(do(nc.tensor.matmul, o.ap[64 * half:64 * half + 64, 128 * qb:128 * qb + 128],
                                               vA[:, k, 64 * kv:64 * kv + 64], pt.ap[:, k, :], start=(k == 0), stop=(k == 3)),
                       t1, ztok["vA", 0], ztok["vA", 1], o.deps, inc=(k == 3))
            pt.done(t)
            if rem == 3:
                t = AC(do(nc.scalar.activation, mix[:, c, :], o.ap[:, 0:256], ACT.Copy), t, after_norm)
                o.done(t)

        ps_ = {0: soft(0)}
        yield
        for n in range(32):
            if n + 1 < 32:
                ps_[n + 1] = soft(n + 1)
            yield from apply(n, ps_.pop(n))
            yield

    def ada_rest():
        for nt in range(16, 48):
            yield from ada(nt)

    filler = ada_rest()

    def limited(g, n):
        for _ in range(n):
            if next(g, "end") == "end":
                return
            yield

    def r_and_gd():
        for n in range(4):
            yield from gemm("w_r", n, range(4), xonly, 1, ev_r(n))
        yield from gemm("w_gd", 0, range(4), [(0, 256 * fb, "B", 32 * fb, HA, 0) for fb in range(2)], 1, ev_gd, w=160,
                        split="tail")

    run_all((attn(), 3), (r_and_gd(), 1))

    f0 = fence()
    rl = counter()
    rwc = A("rwc")
    AC.dma(rwc, io["rwkv_c"], rl, f0)
    wup, aup, w0r = A("wup"), A("aup"), A("w0r")
    AC.dma(wup, io["w_up"], rl, f0)
    AC.dma(aup, io["a_up"], rl, f0)
    for d in range(2):
        rl_tok = AC.dma(w0r[64 * d:64 * d + 1, :], io["w0"][d:d + 1, :], rl, f0)
    kk = A("kk")
    kkc, kac, rkc = cst("k_k", 8), cst("k_a", 8), cst("r_k", 8)
    a0c = cst("a0", 16)
    i64 = rwc[:, 1408:1472]

    def fc(ap):
        return ap.rearrange("p (c n) -> p c n", c=8)

    lwb, Pex, Pin, Pinv, ab, tb_, kd, bh, kh = (A(n) for n in ("lw", "Pex", "Pin", "Pinv", "ab", "tb", "kd", "bh", "kh"))
    sets = [{n: A(n + p) for n in ("ar", "BTA", "AKA", "X", "Xt", "btok", "ktok", "vtok")} for p in "01"]
    T1, R, U, Zs, pcs = A("T1"), A("R"), A("U"), [A("Z0"), A("Z1")], [cols[:, 8 * d:8 * d + 8] for d in range(2)]
    yT = mix[:, 8:16, :]

    def bc(ap, n, m):
        return ap.unsqueeze(1).to_broadcast([128, n, m])

    def bcol(ap, n, m):
        return ap.unsqueeze(2).to_broadcast([128, n, m])

    wd_tok = AC(do(nc.scalar.activation, wdad[:, 0, :], wdad[:, 0, :], ACT.Tanh), ztok["wa", 0], f0)
    kk_tok = []
    for c in range(8):
        kt = ztok[("k", c // 2), c % 2]
        t = DVE(do(nc.vector.tensor_scalar, kk[:, c, :], kT[:, c, :], kkc[:, c:c + 1], None, MUL), kt, f0, const_tok)
        s = A("BTA0") if c % 2 else A("AKA0")
        sq = s.rearrange("p c n -> p (c n)")[:, 0:512]
        t1 = AC(do(nc.scalar.activation, sq, kk[:, c, :], ACT.Square), t, kk_tok[c - 2:c - 1] if c > 1 else None, f0)
        b = X.get()
        t2 = PE(do(nc.tensor.matmul, b.ap, blk, sq, start=True, stop=True), t1, b.deps)
        t3 = DVE(do(nc.vector.tensor_scalar, sq, b.ap, 1e-12, None, MAX), t2)
        b.done(t3)
        t4 = AC(do(nc.scalar.activation, sq, sq, ACT.Sqrt), t3)
        t5 = DVE(do(nc.vector.reciprocal, sq, sq), t4)
        kk_tok.append(DVE(do(nc.vector.tensor_tensor, kk[:, c, :], kk[:, c, :], sq, MUL), t5))

    its = [(d, n) for n in range(8) for d in range(2)]
    free = {}
    done = [[], []]
    state, z_tok, u_read, r_read = {}, [None, None], [], []
    y_tok = {}
    fr = fence()

    def heads(fn, *deps):
        for c in range(8):
            for hh in range(2):
                t = PE(fn(slice(64 * hh, 64 * hh + 64), c), *deps, inc=(c == 7 and hh == 1))
        return t

    def prepare(i):
        d, n = its[i]
        q = sets[i % 2]
        ck = n if d == 0 else (3 - n if n < 4 else 11 - n)
        lat = ck >= 4
        o = 704 * d
        pair, tri = rwc[:, o + 448:o + 576], rwc[0:64, o + 576:o + 704]
        h, tk, tx = slice(64 * d, 64 * d + 64), slice(64 * ck, 64 * ck + 64), slice(64 * (ck - 4), 64 * (ck - 4) + 64)
        old = [done[i % 2], fr]
        b2 = two(G)
        for j in range(2):
            PE(do(nc.tensor.matmul, b2.ap[0:64, 512 * j:512 * j + 512], wdad[h, 0, tk], wup[h, 512 * j:512 * j + 512],
                  start=True, stop=False), wd_tok, rl_tok, b2.deps, inc=False)
            t = PE(do(nc.tensor.matmul, b2.ap[0:64, 512 * j:512 * j + 512], ones[64 * d:64 * d + 1, 0:64],
                      w0r[64 * d:64 * d + 1, 512 * j:512 * j + 512], start=False, stop=True), rl_tok, inc=(j == 1))
        lw = lwb[0:64, :]
        t = tanh_half(lw, b2.ap[0:64, :], t, free.get("lw"), fr)
        b2.done(t)
        lw_tok = DVE(do(nc.vector.tensor_scalar, lw, lw, 1.0, -0.5 * DECAY, ADD, MUL), t)
        yield
        ba = G.get()
        for c in range(8):
            t = PE(do(nc.tensor.matmul, ba.ap[:, 64 * c:64 * c + 64], aup[h, 128 * c:128 * c + 128], wdad[h, 1, tk],
                      start=True, stop=True), ztok["wa", 1], rl_tok, ba.deps, inc=(c == 7))
        t = DVE(do(nc.vector.tensor_tensor, fc(ab), fc(ba.ap), bcol(a0c[:, 8 * d:8 * d + 8], 8, 64), ADD), t, free.get("ab"), fr)
        ba.done(t)
        t = tanh_half(ab, ab, t)
        a_tok = DVE(do(nc.vector.tensor_scalar, ab, ab, 0.5, 0.5, MUL, ADD), t)
        yield
        bv = G.get()
        t = heads(lambda s, c: do(nc.tensor.matmul, bv.ap[s, 64 * c:64 * c + 64], vT[s, c, tk], ident[s, s], start=True, stop=True),
                  bv.deps, [ztok[("v", c // 2), c % 2] for c in range(8)])
        vt_tok = AC(do(nc.scalar.activation, q["vtok"], bv.ap, ACT.Copy), t, old)
        bv.done(vt_tok)
        yield
        b2 = two(G)
        for c in range(8):
            t = PE(do(nc.tensor.matmul, b2.ap[:, 128 * c:128 * c + 128], lw[:, 128 * c:128 * c + 128], tri,
                      start=True, stop=True), lw_tok, b2.deps, inc=(c == 7))
        free["lw"] = [t]
        L = b2.ap.rearrange("p (c n) -> p c n", c=8)
        t3 = AC(do(nc.scalar.activation, fc(Pinv), L[:, :, 0:64], ACT.Exp, scale=-1.0), t, free.get("Pinv"), fr)
        t2 = AC(do(nc.scalar.activation, fc(Pex), L[:, :, 64:128], ACT.Exp), t, free.get("Pex"), fr)
        t1 = AC(do(nc.scalar.activation, fc(Pin), L[:, :, 0:64], ACT.Exp), t, free.get("Pin"), fr)
        b2.done(t1)
        kv, kkv = kT[:, :, tk], kk[:, :, tk]
        u = DVE(do(nc.vector.scalar_tensor_tensor, fc(tb_), fc(ab), -1.0, bcol(kac, 8, 64), ADD, MUL), a_tok, free.get("tb"), fr)
        kd_tok = DVE(do(nc.vector.scalar_tensor_tensor, fc(kd), fc(tb_), 1.0, kv, ADD, MUL), u, free.get("kd"), fr)
        u = PO(do(nc.gpsimd.tensor_tensor, fc(tb_), kkv, fc(ab), MUL), a_tok, kd_tok, kk_tok)
        free["ab"] = [u]
        yield
        kh_tok = DVE(do(nc.vector.tensor_tensor, kh, kd, Pinv, MUL), kd_tok, t3, free.get("kh"), fr)
        free["kd"] = [kh_tok]
        ar = q["ar"]
        ar_tok = [DVE(do(nc.vector.scalar_tensor_tensor, ar[:, :, 0:64], kkv, -1.0, fc(Pex), MUL, MUL), t2, kk_tok, old)]
        free["Pex"] = ar_tok[0:1]
        if lat:
            ar_tok.append(PO(do(nc.gpsimd.tensor_tensor, ar[:, :, 64:128], rT[:, :, tx], fc(Pin), MUL), t1,
                             [ztok["r", c] for c in range(8)], old))
        bh_tok = DVE(do(nc.vector.tensor_tensor, bh, tb_, Pinv, MUL), u, t3, free.get("bh"), fr)
        free["tb"] = free["Pinv"] = [bh_tok]
        pc_tok = DVE(do(nc.vector.tensor_copy, pcs[i % 2], fc(Pin)[:, :, 63 if d == 0 else 0]), t1, old)
        free["Pin"] = [pc_tok] + ar_tok[1:]
        yield

        def turn(dst, src, *deps):
            b = G.get()
            t = heads(lambda s, c: do(nc.tensor.matmul, b.ap[s, 64 * c:64 * c + 64], fc(src)[s, c, :], ident[s, s], start=True, stop=True),
                      b.deps, *deps)
            t = AC(do(nc.scalar.activation, dst, b.ap, ACT.Copy), t, old)
            b.done(t)
            return t

        w = 128 if lat else 64

        def pairs(dst, lhs, *deps):
            b = two(G)
            bv = b.ap.rearrange("p (c n) -> p c n", c=8)
            t = heads(lambda s, c: do(nc.tensor.matmul, bv[s, c, 0:w], fc(lhs)[s, c, :], ar[s, c, 0:w], start=True, stop=True),
                      b.deps, ar_tok, *deps)
            t = DVE(do(nc.vector.tensor_tensor, dst[:, :, 0:w], bv[:, :, 0:w], bc(pair[:, 0:w], 8, w), MUL), t, old)
            b.done(t)
            return t

        kt_tok = turn(q["ktok"], kh, kh_tok)
        yield
        bta_tok = pairs(q["BTA"], bh, bh_tok)
        yield
        b = G.get()
        t = heads(lambda s, c: do(nc.tensor.matmul, b.ap[s, 64 * c:64 * c + 64], ar[s, c, 0:64], fc(bh)[s, c, :], start=True, stop=True),
                  b.deps, ar_tok, bh_tok)
        t = DVE(do(nc.vector.tensor_tensor, fc(q["X"]), fc(b.ap), bc(rwc[:, o:o + 64], 8, 64), MUL), t, old)
        b.done(t)
        x_t = DVE(do(nc.vector.tensor_tensor, fc(q["X"]), fc(q["X"]), bc(i64, 8, 64), ADD), t)
        t = DVE(do(nc.vector.tensor_tensor, fc(q["Xt"]), q["BTA"][:, :, 0:64], bc(rwc[:, o + 384:o + 448], 8, 64), MUL), bta_tok, old)
        xt_t = PO(do(nc.gpsimd.tensor_tensor, fc(q["Xt"]), fc(q["Xt"]), bc(i64, 8, 64), ADD), t)
        yield
        bt_tok = turn(q["btok"], bh, bh_tok)
        free["bh"] = [bt_tok]
        yield
        aka_tok = pairs(q["AKA"], kh, kh_tok)
        free["kh"] = [aka_tok]
        state[i] = dict(bta=bta_tok, aka=aka_tok, x=x_t, xt=xt_t, vt=vt_tok, kt=kt_tok, bt=bt_tok, ar=ar_tok, pc=pc_tok)
        yield

    sl = [slice(64 * c, 64 * c + 64) for c in range(8)]

    def solve(i):
        d, n = its[i]
        q, k = sets[i % 2], state[i]
        Xb, Xt, BTA, AKA, ar, vtok = (q[m] for m in ("X", "Xt", "BTA", "AKA", "ar", "vtok"))
        x_t, xt_t = k["x"], k["xt"]
        first, last, Z = n == 0, n == 7, Zs[d]
        lat = n >= 4
        ck = n if d == 0 else (3 - n if n < 4 else 11 - n)
        for lv in range(1, 6):
            mask = rwc[:, 704 * d + 64 * lv:704 * d + 64 * lv + 64]
            b = X.get()
            t = heads(lambda s, c: do(nc.tensor.matmul, b.ap[s, sl[c]], BTA[s, c, 0:64], fc(Xb)[s, c, :], start=True, stop=True),
                      b.deps, k["bta"], x_t)
            t1_t = DVE(do(nc.vector.tensor_tensor, fc(T1), fc(b.ap), bc(mask, 8, 64), MUL), t, xt_t, fr)
            b.done(t1_t)
            yield
            if lv < 5:
                bx = X.get()
                t = heads(lambda s, c: do(nc.tensor.matmul, bx.ap[s, sl[c]], fc(Xt)[s, c, :], fc(T1)[s, c, :], start=True, stop=True),
                          bx.deps, t1_t, xt_t)
                x_t = DVE(do(nc.vector.tensor_tensor, Xb, Xb, bx.ap, ADD), t)
                bx.done(x_t)
            by = X.get()
            t = heads(lambda s, c: do(nc.tensor.matmul, by.ap[s, sl[c]], fc(T1)[s, c, :], fc(Xt)[s, c, :], start=True, stop=True),
                      by.deps, t1_t, xt_t)
            xt_t = DVE(do(nc.vector.tensor_tensor, Xt, Xt, by.ap, ADD), t)
            by.done(xt_t)
            yield
        b = X.get()
        for c in range(8):
            for hh in range(2):
                s = slice(64 * hh, 64 * hh + 64)
                if not first:
                    PE(do(nc.tensor.matmul, b.ap[s, sl[c]], ar[s, c, 0:64], fc(Z)[s, c, :], start=True, stop=False,
                          skip_group_check=True), b.deps, k["ar"], z_tok[d], inc=False)
                t = PE(do(nc.tensor.matmul, b.ap[s, sl[c]], AKA[s, c, 0:64], fc(vtok)[s, c, :], start=first, stop=True,
                          skip_group_check=True), b.deps, k["aka"], k["vt"], inc=(c == 7 and hh == 1))
        r_tok = AC(do(nc.scalar.activation, R, b.ap, ACT.Copy), t, r_read, fr)
        b.done(r_tok)
        yield
        b = X.get()
        t = heads(lambda s, c: do(nc.tensor.matmul, b.ap[s, sl[c]], fc(Xt)[s, c, :], fc(R)[s, c, :], start=True, stop=True),
                  b.deps, xt_t, r_tok)
        r_read[:] = [t]
        u_tok = AC(do(nc.scalar.activation, U, b.ap, ACT.Copy), t, u_read, fr)
        b.done(u_tok)
        yield
        if not last:
            b = X.get()
            for c in range(8):
                for hh in range(2):
                    s = slice(64 * hh, 64 * hh + 64)
                    PE(do(nc.tensor.matmul, b.ap[s, sl[c]], fc(q["btok"])[s, c, :], fc(U)[s, c, :], start=True, stop=False,
                          skip_group_check=True), b.deps, k["bt"], u_tok, inc=False)
                    t = PE(do(nc.tensor.matmul, b.ap[s, sl[c]], fc(q["ktok"])[s, c, :], fc(vtok)[s, c, :], start=False,
                              stop=True, skip_group_check=True), k["kt"], k["vt"], inc=(c == 7 and hh == 1))
            zb, zt = b, t
        if lat:
            tx = slice(64 * (ck - 4), 64 * (ck - 4) + 64)
            b = X.get()
            for c in range(8):
                for hh in range(2):
                    s = slice(64 * hh, 64 * hh + 64)
                    PE(do(nc.tensor.matmul, b.ap[s, sl[c]], fc(Z)[s, c, :], ar[s, c, 64:128], start=True, stop=False,
                          skip_group_check=True), b.deps, z_tok[d], k["ar"], inc=False)
                    PE(do(nc.tensor.matmul, b.ap[s, sl[c]], fc(U)[s, c, :], BTA[s, c, 64:128], start=False, stop=False,
                          skip_group_check=True), u_tok, inc=False)
                    t = PE(do(nc.tensor.matmul, b.ap[s, sl[c]], fc(vtok)[s, c, :], AKA[s, c, 64:128], start=False,
                              stop=True, skip_group_check=True), k["aka"], k["vt"], inc=(c == 7 and hh == 1))
            if ck not in y_tok:
                y_tok[ck] = AC(do(nc.scalar.activation, yT[:, :, tx], fc(b.ap), ACT.Copy), t, fr)
            else:
                y_tok[ck] = DVE(do(nc.vector.tensor_tensor, yT[:, :, tx], yT[:, :, tx], fc(b.ap), ADD), t, y_tok[ck])
            b.done(y_tok[ck])
        u_read[:] = [t]
        if not last:
            pc = bcol(pcs[i % 2], 8, 64)
            if first:
                z_tok[d] = DVE(do(nc.vector.tensor_tensor, fc(Z), fc(zb.ap), pc, MUL), zt, k["pc"], fr)
                zb.done(z_tok[d])
            else:
                z1 = DVE(do(nc.vector.tensor_tensor, Z, Z, zb.ap, ADD), zt, t)
                zb.done(z1)
                z_tok[d] = DVE(do(nc.vector.tensor_tensor, fc(Z), fc(Z), pc, MUL), z1, k["pc"])
        done[i % 2] = [t, z_tok[d], xt_t, x_t]
        yield

    rest(prepare(0))
    for i in range(16):
        run_all((solve(i), 1), (prepare(i + 1) if i < 15 else iter(()), 1), (limited(filler, 16), 1))
    rest(filler)

    f1 = fence()
    gl = counter()
    gup, gup2 = A("gup"), A("gup2")
    AC.dma(gup, io["g_up"][0:128, :], gl, f1)
    gl_tok = AC.dma(gup2[96:128, :], io["g_up"][128:160, :], gl, f1)
    s8 = [A("s8a"), A("s8b")]
    lng, lnb = cst("lnx_g", 8), cst("lnx_b", 8)
    sfree = [f1, f1]
    for c in range(8):
        y = yT[:, c, :]
        s = s8[c % 2]
        mu, sq, rk, g = (s[:, 256 * i:256 * i + 256] for i in range(4))
        ff = sfree[c % 2]
        b = X.get()
        m = PE(do(nc.tensor.matmul, b.ap[:, 0:256], blk, y, start=True, stop=True), f1, b.deps)
        t = DVE(do(nc.vector.scalar_tensor_tensor, y, b.ap[:, 0:256], -1.0 / 64, y, MUL, ADD), m)
        t1 = AC(do(nc.scalar.activation, sq, y, ACT.Square), t, ff)
        m = PE(do(nc.tensor.matmul, b.ap[:, 256:512], blk, sq, start=True, stop=True), t1)
        t2 = DVE(do(nc.vector.tensor_scalar, mu, b.ap[:, 256:512], 1.0 / 64, 64e-5, MUL, ADD), m, ff)
        b.done(t2)
        t2 = AC(do(nc.scalar.activation, mu, mu, ACT.Sqrt), t2)
        t2 = DVE(do(nc.vector.reciprocal, mu, mu), t2)
        t2 = DVE(do(nc.vector.scalar_tensor_tensor, y, y, lng[:, c:c + 1], mu, MUL, MUL), t2)
        yn = DVE(do(nc.vector.tensor_scalar, y, y, lnb[:, c:c + 1], None, ADD), t2)
        b, b2 = X.get(), X.get()
        for d, bd in enumerate((b, b2)):
            h = slice(64 * d, 64 * d + 64)
            m = PE(do(nc.tensor.matmul, bd.ap[:, 0:256], aup[h, 128 * c:128 * c + 128], wdad[h, 1, 256:512],
                                      start=True, stop=True), bd.deps, inc=(d == 1))
        t0 = DVE(do(nc.vector.tensor_scalar, rk, b.ap[:, 0:256], a0c[:, c:c + 1], None, ADD), m, ff)
        t1 = DVE(do(nc.vector.tensor_scalar, g, b2.ap[:, 0:256], a0c[:, 8 + c:9 + c], None, ADD), m, ff)
        b.done(t0)
        b2.done(t1)
        t0 = tanh_half(rk, rk, t0)
        t1 = tanh_half(g, g, t1)
        t = DVE(do(nc.vector.tensor_tensor, rk, rk, g, ADD), t0, t1)
        t = DVE(do(nc.vector.tensor_scalar, rk, rk, 0.5, -1.0, MUL, ADD), t)
        t = DVE(do(nc.vector.tensor_scalar, rk, rk, kac[:, c:c + 1], 2.0, MUL, ADD), t)
        t = DVE(do(nc.vector.tensor_tensor, rk, rk, kT[:, c, 256:512], MUL), t)
        t = DVE(do(nc.vector.scalar_tensor_tensor, rk, rk, rkc[:, c:c + 1], rT[:, c, :], MUL, MUL), t)
        b = X.get()
        m = PE(do(nc.tensor.matmul, b.ap[:, 0:256], blk, rk, start=True, stop=True), t, b.deps)
        t = DVE(do(nc.vector.tensor_tensor, rk, b.ap[:, 0:256], vT[:, c, 256:512], MUL), m)
        t = DVE(do(nc.vector.tensor_tensor, y, y, rk, ADD), t, yn)
        PE(do(nc.tensor.matmul, b.ap[:, 256:512], gup[:, 128 * c:128 * c + 128], gd[:, 0, :], start=True, stop=False,
                                        skip_group_check=True), gl_tok, t, ztok["gd", 0], inc=False)
        m = PE(do(nc.tensor.matmul, b.ap[:, 256:512], gup2[96:128, 128 * c:128 * c + 128], gd[96:128, 1, :], start=False,
                                            stop=True, skip_group_check=True), ztok["gd", 1])
        t = DVE(do(nc.vector.tensor_tensor, y, y, b.ap[:, 256:512], MUL), m, t)
        b.done(t)
        sfree[c % 2] = [t]

    f2 = fence()
    open_gate(f2)
    xl = counter()
    x_tok = AC.dma(xt, io["xT"], xl, f2)
    HA.tok = [[] for _ in range(16)]
    for c in range(0, 16, 4):
        split(HA, c, 4, mix[:, c:c + 4, :], f2)

    xdeps = {}

    def add_to_x(gate, gtok):
        def make(n):
            def ev(banks, tok):
                for fb in range(2):
                    c = 2 * n + fb
                    if gate is None:
                        t = DVE(do(nc.vector.tensor_tensor, xt[:, c, :], xt[:, c, :],
                                                                     banks[0].ap[:, 256 * fb:256 * fb + 256], ADD),
                                tok, x_tok, xdeps.get(c))
                    else:
                        t = DVE(do(nc.vector.scalar_tensor_tensor, xt[:, c, :], banks[0].ap[:, 256 * fb:256 * fb + 256], gate[:, c:c + 1], xt[:, c, :], MUL, ADD),
                            tok, x_tok, gtok, xdeps.get(c))
                    xdeps[c] = t
                banks[0].done(t)
            return ev
        return make

    ev = add_to_x(mods[:, 2, 0, :], mod_tok[23])
    for n in range(8):
        rest(gemm("w_out", n, range(4), xonly, 1, ev(n)))
    g2s = plus_one(gs[:, 0:16], cst("norm2", 16), mods[:, 4, 0, :], mod_tok[39], fence())
    r = rms(xt, 16, list(xdeps.values()), work4)
    normed(xt, r, gs[:, 0:16], mods[:, 3, 0, :], HA, [g2s, mod_tok[31], fence()])

    ev_x = add_to_x(mods[:, 5, 0, :], mod_tok[47])
    bon = [(0, 256 * fb, "B", 128 * fb, HB, 0) for fb in range(2)]

    def swiglu(gate_up, pos):
        (a, ta), (b, tb) = gate_up
        s = work4.get()
        th, v = (s.ap[:, 2 * i:2 * i + 2, :] for i in range(2))
        av, bv = (q.ap.rearrange("p (c n) -> p c n", c=2) for q in (a, b))
        t = tanh_half(th, av, ta, s.deps)
        t = DVE(do(nc.vector.scalar_tensor_tensor, v, th, 1.0, av, ADD, MUL), t)
        a.done(t)
        t = DVE(do(nc.vector.scalar_tensor_tensor, v, v, 0.5, bv, MUL, MUL), t, tb)
        b.done(t)
        s.done(split(HB, pos, 2, v, t, hb_dep))

    held = {}

    def keep(name):
        def ev(banks, tok):
            held[name] = (banks[0], tok)
        return ev

    for part, (k0, k1) in enumerate(((0, 4), (4, 8), (8, 11))):
        hb_dep = [PE.last()]
        for j in range(2 * k0, 2 * k1):
            rest(gemm("ffn1", j, range(4), xonly, 1, keep("a")))
            rest(gemm("ffn3", j, range(4), xonly, 1, keep("b")))
            swiglu((held["a"], held["b"]), 2 * (j - 2 * k0))
        for n in range(8):
            rest(gemm("ffn2", n, range(k0, k1), bon, 1, ev_x(n), kbase=k0))

    def norm_in_place(gain, xdone):
        r = rms(xt, 16, xdone, work4)
        toks = []
        for c in range(16):
            toks.append(DVE(do(nc.vector.scalar_tensor_tensor, xt[:, c, :], xt[:, c, :], gain[:, c:c + 1], r.ap, MUL, MUL),
                            r.tok, xdone))
        r.done(toks)
        for c in range(16):
            xdeps[c] = toks[c]
        return toks

    norm_in_place(cst("final1", 16), [list(xdeps.values()), fence()])

    work2 = None

    def silu_from(dst, bank, tok, *deps):
        b = bank.ap.rearrange("p (c n) -> p c n", c=2)
        t = tanh_half(dst, b, tok, *deps)
        t = DVE(do(nc.vector.scalar_tensor_tensor, dst, dst, 1.0, b, ADD, MUL), t)
        bank.done(t)
        return DVE(do(nc.vector.tensor_scalar, dst, dst, 0.5, None, MUL), t)

    def tile(pool, name, nt, kind, acts, finish):
        box = {}

        def ev(banks, tok):
            b = pool.get()
            box["b"] = b
            b.tok = finish(b.ap, banks[0], tok, b.deps)
        outs = [(0, 256 * i, kind, 128 * i if kind == "B" else 0, acts, i) for i in range(2)]
        return box, gemm(name, nt, range(4), outs, 1, ev)

    def plain(scale=1.0):
        def f(dst, bank, tok, deps):
            t = AC(do(nc.scalar.activation, dst, bank.ap.rearrange("p (c n) -> p c n", c=2), ACT.Copy, scale=scale), tok, deps)
            bank.done(t)
            return t
        return f

    def gated(dst, bank, tok, deps):
        return silu_from(dst, bank, tok, deps)

    def softmax_rows(p, width, scale, k, *deps):
        mx, nm, rs = (cols[:, k + i:k + i + 1] for i in range(3))
        t = DVE(do(nc.vector.tensor_reduce, mx, p, AX.X, MAX), *deps)
        t = DVE(do(nc.vector.tensor_scalar, nm, mx, -scale, None, MUL), t)
        t = AC(do(nc.scalar.activation, p, p, ACT.Exp, bias=nm, scale=scale, accum_out=rs), t)
        t = DVE(do(nc.vector.reciprocal, rs, rs), t)
        return DVE(do(nc.vector.tensor_scalar, p, p, rs, None, MUL), t)

    def mem_head(q, k, v, g, ch, pool, big):
        b = X.get()
        for qb in range(2):
            for dc in range(2):
                t = PE(do(nc.tensor.matmul, b.ap[:, 256 * qb:256 * qb + 256], q.ap[:, dc, 128 * qb:128 * qb + 128],
                                                        k.ap[:, dc, :], start=(dc == 0), stop=(dc == 1)),
                       q.tok, k.tok, b.deps, inc=(qb == 1 and dc == 1))
        p = big.get()
        t1 = AC(do(nc.scalar.activation, p.ap[:, 0:512], b.ap, ACT.Copy), t, p.deps)
        b.done(t1)
        yield
        tt = [softmax_rows(p.ap[:, 256 * qb:256 * qb + 256], 256, 1.0 / 16, 8 * qb + 4 * (ch % 4), t1) for qb in range(2)]
        b = X.get()
        for qb in range(2):
            for mb in range(2):
                t = PE(do(nc.tensor.transpose, b.ap[:, 256 * mb + 128 * qb:256 * mb + 128 * qb + 128],
                                                           p.ap[:, 256 * qb + 128 * mb:256 * qb + 128 * mb + 128], ident),
                       tt, b.deps, inc=(qb == 1 and mb == 1))
        t1 = AC(do(nc.scalar.activation, p.ap[:, 0:512], b.ap, ACT.Copy), t)
        b.done(t1)
        yield
        b = X.get()
        for dc in range(2):
            for mb in range(2):
                t = PE(do(nc.tensor.matmul, b.ap[:, 256 * dc:256 * dc + 256], v.ap[:, mb, 128 * dc:128 * dc + 128],
                                                        p.ap[:, 256 * mb:256 * mb + 256], start=(mb == 0), stop=(mb == 1)),
                       t1, v.tok, b.deps, inc=(dc == 1 and mb == 1))
        p.done(t)
        t2 = DVE(do(nc.vector.tensor_tensor, mix[:, ch:ch + 2, :], b.ap.rearrange("p (c n) -> p c n", c=2), g.ap, MUL), t, g.tok, mix_dep)
        b.done(t2)
        q.done(t)
        k.done(t)
        v.done(t)
        g.done(t2)
        yield

    def pipeline(groups, ratio=1):
        before = None
        for tiles, after in groups:
            def products():
                for _, g in tiles:
                    yield from g
            if before is None:
                rest(products())
            else:
                run_all((products(), ratio), (before, 1))
            before = after([b["b"] for b, _ in tiles])
        return before

    l_mem = [counter() for _ in range(4)]

    def recall(pool, lay, n, i):
        box = {}

        def load():
            b = pool.get()
            box["b"] = b
            b.tok = AC.dma(b.ap, io["mem_keep"][lay, n].rearrange("p (c n) -> p c n", c=2), l_mem[i], b.deps, mem_saved[lay, n])
            yield
        return box, load()

    def mem_groups(lay, wname, q0, g0, pool, big):
        res = []
        for h in range(4):
            tiles = [recall(pool, lay, h, h % 2), recall(pool, lay, 4 + h, 2 + h % 2),
                     tile(pool, wname, q0 + h, "B", HA, plain()), tile(pool, wname, g0 + h, "B", HA, gated)]
            res.append((tiles, lambda bs, h=h: mem_head(bs[2], bs[0], bs[1], bs[3], 16 + 2 * h, pool, big)))
        return res

    def pool2(name, n):
        v = A(name)
        return Pool([v[:, 512 * i:512 * i + 512].rearrange("p (c n) -> p c n", c=2) for i in range(n)])

    f3 = fence()
    r = rms(xt, 16, list(xdeps.values()), work4)
    normed(xt, r, cst("norm_a", 16), None, HA, f3)
    f4 = fence()
    mix_dep = f4
    pl = counter()
    pl_tok = AC.dma(phc[:, 0:512], io["ret_c"], pl, f4)
    cos2, sin2 = phc[:, 0:256], phc[:, 256:512]
    dec = Pool([phc[:, 512 + 512 * i:1024 + 512 * i] for i in range(2)])
    for i in range(2):
        dec.free[i] = (i, [f4])
    dsem = [counter(), counter()]
    w2 = pool2("work", 11)
    big = Pool([A("work")[:, 5632 + 1024 * i:5632 + 1024 * i + 1024] for i in range(2)])
    for pool in (w2, big):
        pool.free = [(i, [f4]) for i, _ in pool.free]

    def rotated(scale):
        def f(dst, bank, tok, deps):
            out_, done = [], []
            dead.append(deps)
            for c in range(2):
                t1, t2 = rope(dst[:, c, :], bank, 256 * c, 256, scale, tok, cst("rot128", 128), cos2, sin2, pl_tok)
                done.append(t1)
                out_.append(t2)
            bank.done(done)
            return out_
        return f

    def ret_head(q, k, v, g, c, h, last):
        db = dec.get()
        d_tok = AC.dma(db.ap, io["decay"][h], dsem[db.i], db.deps)
        b = X.get()
        for kb in range(2):
            t = PE(do(nc.tensor.matmul, b.ap[:, 256 * kb:256 * kb + 256], k.ap[:, c, 128 * kb:128 * kb + 128], q.ap[:, c, :],
                                             start=True, stop=True), q.tok, k.tok, b.deps, inc=(kb == 1))
        s = big.get()
        t1 = DVE(do(nc.vector.tensor_tensor, s.ap[:, 0:512], b.ap, db.ap, MUL), t, d_tok, s.deps)
        b.done(t1)
        db.done(t1)
        yield
        b = X.get()
        for ec in range(2):
            for kb in range(2):
                t2 = PE(do(nc.tensor.matmul, b.ap[:, 256 * ec:256 * ec + 256], v.ap[:, kb, 128 * ec:128 * ec + 128],
                                                         s.ap[:, 256 * kb:256 * kb + 256], start=(kb == 0), stop=(kb == 1)),
                        t1, v.tok, b.deps, inc=(ec == 1 and kb == 1))
        o = mix[:, 2 * h:2 * h + 2, :]
        bv = b.ap.rearrange("p (c n) -> p c n", c=2)
        ta = AC(do(nc.scalar.activation, s.ap[:, 512:1024], b.ap, ACT.Square), t2)
        yield
        b2 = X.get()
        for ec in range(2):
            t = PE(do(nc.tensor.matmul, b2.ap[:, 0:256], ones, s.ap[:, 512 + 256 * ec:768 + 256 * ec], start=(ec == 0), stop=(ec == 1)),
                   ta, b2.deps, inc=(ec == 1))
        rr = s.ap[:, 0:256]
        t = DVE(do(nc.vector.tensor_scalar, rr, b2.ap[:, 0:256], 1.0 / 256, 1e-6, MUL, ADD), t, t2)
        b2.done(t)
        t = AC(do(nc.scalar.activation, rr, rr, ACT.Sqrt), t)
        t = DVE(do(nc.vector.reciprocal, rr, rr), t)
        t = DVE(do(nc.vector.tensor_tensor, o, bv, rr.unsqueeze(1).to_broadcast([128, 2, 256]), MUL), t, mix_dep)
        b.done(t)
        s.done(t)
        t = PO(do(nc.gpsimd.tensor_tensor, o, o, g.ap, MUL), t, g.tok)
        v.done(t2)
        g.done(t)
        if last:
            q.done(t2)
            k.done(t2)
        yield

    groups = mem_groups(0, "w_in_a", 24, 28, w2, big)
    for p in range(4):
        tiles = [tile(w2, "w_in_a", p, "B", HA, rotated(1.0)), tile(w2, "w_in_a", 4 + p, "B", HA, rotated(128 ** -0.5)),
                 tile(w2, "w_in_a", 8 + 2 * p, "A", HA, plain()), tile(w2, "w_in_a", 16 + 2 * p, "B", HA, gated),
                 tile(w2, "w_in_a", 9 + 2 * p, "A", HA, plain()), tile(w2, "w_in_a", 17 + 2 * p, "B", HA, gated)]

        def heads2(bs, p=p):
            q, k, v0, g0, v1, g1 = bs
            yield from ret_head(q, k, v0, g0, 0, 2 * p, False)
            yield from ret_head(q, k, v1, g1, 1, 2 * p + 1, True)
        groups.append((tiles, heads2))
    rest(pipeline(groups, 2))

    def project(name):
        f = fence()
        for c in range(0, 16, 4):
            split(HA, c, 4, mix[:, c:c + 4, :], f)
        for c in range(0, 8, 4):
            split(HB, c, 4, mix[:, 16 + c:20 + c, :], f)
        wide = Wide(HA, HB)
        ev = add_to_x(None, None)
        for n in range(8):
            rest(gemm(name, n, range(6), [(0, 256 * fb, "B", 128 * fb, wide, 0) for fb in range(2)], 1, ev(n)))

    class Wide:
        def __init__(self, a, b):
            self.hi, self.lo = Pick(a.hi, b.hi), Pick(a.lo, b.lo)
            self.tok = a.tok + b.tok

    class Pick:
        def __init__(self, a, b):
            self.a, self.b = a, b

        def __getitem__(self, key):
            p, c, n = key
            return self.a[p, c, n] if c < 16 else self.b[p, c - 16, n]

    project("w_out_a")

    f5 = fence()
    r = rms(xt, 16, list(xdeps.values()), work4_after(f5, work4))
    normed(xt, r, cst("norm_b", 16), None, HA, f5)
    f6 = fence()
    mix_dep = f6
    for pool in (w2, big):
        pool.free = [(i, [f6]) for i, _ in pool.free]
    rest(pipeline(mem_groups(1, "w_in_b", 32, 36, w2, big)))
    f7 = fence()
    r = rms(xt, 16, list(xdeps.values()), work4_after(f7, work4))
    normed(xt, r, cst("kv_g", 16), None, HB, f7)
    f8 = fence()
    xs = counter()
    xs_tok = AC.dma(io["x_keep"], xt, xs, f8)
    pl = counter()
    pm_tok = AC.dma(phc[:, 0:1152], io["dil_c"], pl, f8)
    w3 = Pool([A("work")[:, 512 * i:512 * i + 512].rearrange("p (c n) -> p c n", c=2) for i in range(15)]
              + [A("xw")[:, 512 * i:512 * i + 512].rearrange("p (c n) -> p c n", c=2) for i in range(2)])
    w3.free = [(i, [f8, xs_tok]) for i, _ in w3.free]
    xw = A("xw")
    pb = Pool([xw[:, 1024:1792], xw[:, 1792:2560]])
    pt9 = Pool([xw[:, 2560:3328], xw[:, 3328:4096]])
    for pool in (pb, pt9):
        pool.free = [(i, [f8, xs_tok]) for i, _ in pool.free]

    def dil_head(qs, ks, vs, g, c, h, last):
        ob = X.get()
        for qb in range(2):
            nk = qb + 1
            w = 128 * nk
            b = two(X) if qb else X.get()
            for gi in range(3):
                t = PE(do(nc.tensor.matmul, b.ap[:, w * gi:w * gi + w], qs[gi].ap[:, c, 128 * qb:128 * qb + 128],
                                                 ks[gi].ap[:, c, 0:w], start=True, stop=True),
                       [q.tok for q in qs], [k.tok for k in ks], b.deps, inc=(gi == 2))
            p = pb.get()
            pv = p.ap[:, 0:3 * w]
            mk = phc[:, 384 * qb:384 * qb + 3 * w]
            t1 = DVE(do(nc.vector.tensor_tensor, pv, b.ap[:, 0:3 * w], mk, ADD), t, p.deps, pm_tok)
            b.done(t1)
            yield
            t2 = softmax_rows(pv, 3 * w, 128 ** -0.5, 4 * ((2 * h + qb) % 8), t1)
            b = two(X) if qb else X.get()
            n = 3 * nk
            for i in range(n):
                t = PE(do(nc.tensor.transpose, b.ap[:, 128 * i:128 * i + 128], pv[:, 128 * i:128 * i + 128], ident),
                       t2, b.deps, inc=(i == n - 1))
            p.done(t)
            pt = pt9.get()
            t1 = AC(do(nc.scalar.activation, pt.ap[:, 0:128 * n], b.ap[:, 0:128 * n], ACT.Copy), t, pt.deps)
            b.done(t1)
            yield
            for i in range(n):
                gi, kb = divmod(i, nk)
                t = PE(do(nc.tensor.matmul, ob.ap[:, 128 * qb:128 * qb + 128], vs[gi].ap[:, kb, 128 * c:128 * c + 128], pt.ap[:, 128 * i:128 * i + 128],
                    start=(i == 0), stop=(i == n - 1)), t1, [v.tok for v in vs], ob.deps, inc=(i == n - 1))
            pt.done(t)
        t2 = DVE(do(nc.vector.tensor_tensor, mix[:, h, :], ob.ap[:, 0:256], g.ap[:, c, :], MUL), t, g.tok, mix_dep)
        ob.done(t2)
        if last:
            for x in qs + ks + vs:
                x.done(t)
            g.done(t2)
        yield

    groups = []
    for p in range(8):
        tiles = [tile(w3, "w_in_b", 8 * gi + p, "B", HA, plain()) for gi in range(3)]
        tiles += [tile(w3, "w_kv", 16 * gi + p, "B", HB, plain()) for gi in range(3)]
        tiles += [tile(w3, "w_kv", 16 * gi + 8 + p, "A", HB, plain()) for gi in range(3)]
        tiles += [tile(w3, "w_in_b", 24 + p, "B", HA, gated)]

        def heads3(bs, p=p):
            for c in range(2):
                yield from dil_head(bs[0:3], bs[3:6], bs[6:9], bs[9], c, 2 * p + c, c == 1)
        groups.append((tiles, heads3))
    rest(pipeline_tight(groups, run_all, rest))
    f9 = fence()
    xr = counter()
    x_tok = AC.dma(xt, io["x_keep"], xr, f9, xs_tok)
    project("w_out_b")
    toks = norm_in_place(cst("final2", 16), [list(xdeps.values()), fence()])
    ol = counter()
    o_tok = SP.dma(out, xt, ol, toks)
    SP.queue.append((SP.waits([o_tok, xs_tok]), None, None, 0))
    return engines, rec


def work4_after(deps, pool):
    pool.free = [(i, [deps]) for i, _ in pool.free]
    return pool


def pipeline_tight(groups, run_all, rest):
    before = None
    for tiles, after in groups:
        def part(ts):
            for _, g in ts:
                yield from g
        if before is None:
            rest(part(tiles))
        else:
            run_all((part(tiles[:7]), 2), (before, 1))
            rest(part(tiles[7:]))
        before = after([b["b"] for b, _ in tiles])
    return before


COLS = {}
NCONST = 0
for _n, _w in (("ident", 128), ("ones", 128), ("blk", 128), ("rot32", 128), ("rot128", 128), ("c", 32), ("ada_b", 96),
               ("norm1", 16), ("norm2", 16), ("final1", 16), ("norm_a", 16), ("norm_b", 16), ("mem_g", 16), ("kv_g", 16),
               ("final2", 16), ("ts", 56), ("a0", 16), ("k_k", 8), ("k_a", 8), ("r_k", 8), ("lnx_g", 8), ("lnx_b", 8),
               ("sink", 16), ("sel", 2)):
    COLS[_n] = NCONST
    NCONST += _w


def memory(nc, base):
    m = {}

    def at(name, off, shape, dt=F32):
        m[name] = nc.alloc_sbuf_tensor_at(name, [128, *shape], dt, offset=base + off)[:]

    K = 1024
    at("raw", 0, [NRAW, 1024])
    at("wh", 24 * K, [NW, 1024], F32R)
    at("wl", 40 * K, [NW, 1024], F32R)
    x, hah, hal, hbh, hbl, mx = 56 * K, 72 * K, 88 * K, 104 * K, 120 * K, 136 * K
    at("x", x, [16, T])
    at("xk", x, [8, 512])
    at("xw", x, [4096])
    at("hah", hah, [16, T], F32R)
    at("hal", hal, [16, T], F32R)
    at("hbh", hbh, [16, T], F32R)
    at("hbl", hbl, [16, T], F32R)
    at("mix", mx, [24, T])
    c = 160 * K
    at("const", c, [NCONST])
    at("mod", c + 4128, [192])
    at("sc", c + 4896, [32])
    at("gs", c + 5024, [32])
    at("tsr", c + 5152, [28])
    at("cols", c + 5280, [64])
    c += 5664
    at("phc", c, [1536])
    at("rwc", c, [1472])
    c += 6144
    at("rst", c, [2, T])
    at("tm", c + 2048, [4, T])
    c += 6144
    at("work", c, [7680])
    wk = c
    at("kk", hah, [8, 512])
    at("hal32", hal, [4096])
    at("hbl32", hbl, [4096])
    for i, (n, w) in enumerate((("lw", 1024), ("Pex", 512), ("Pin", 512), ("Pinv", 512), ("ab", 512), ("tb", 512), ("kd", 512))):
        at(n, hal + (0 if i == 0 else 4096 + 2048 * (i - 1)), [w])
    at("wup", hbl, [1024])
    at("aup", hbl + 4096, [1024])
    at("w0r", hbl + 8192, [1024])
    at("bh", hbl + 12288, [512])
    at("kh", hbl + 14336, [512])
    at("hb_r", hbh, [8, T])
    at("hb_q", hbh + 8192, [8, T])
    for n, o, w in (("btok", hbh + 8192, [512]), ("ktok", hbh + 10240, [512]), ("vtok", hbh + 12288, [512]), ("X", hbh + 14336, [512]),
                    ("ar", wk + 16384, [8, 128]), ("BTA", wk + 20480, [8, 128]), ("AKA", mx + 16 * K, [8, 128]),
                    ("Xt", mx + 20 * K, [512])):
        at(n + "0", o, w)
    for n, o, w in (("ar", 24, [8, 128]), ("BTA", 28, [8, 128]), ("AKA", 32, [8, 128]), ("X", 36, [512]), ("Xt", 38, [512]),
                    ("btok", 40, [512]), ("ktok", 42, [512]), ("vtok", 44, [512])):
        at(n + "1", o * K, w)
    for n, o in (("T1", 46), ("R", 48), ("U", 50), ("Z0", 52), ("Z1", 54)):
        at(n, o * K, [512])
    at("sc16", mx + 22 * K, [512])
    at("gup", hah, [1024])
    at("gup2", hah + 4096, [1024])
    at("s8a", hal, [1024])
    at("s8b", hal + 4096, [1024])
    assert wk + 7680 * 4 + base <= 229344, wk + 7680 * 4 + base
    return m


def bass_program(nc, io, out):
    with ExitStack() as ctx:
        sems = {n: ctx.enter_context(nc.semaphore(n)) for n in [f"e{i}" for i in range(5)] + [f"d{i}" for i in range(60)]}
        base = -(-nc.sbuf_base // 32) * 32
        mem = memory(nc, base)
        mem["ps"] = ctx.enter_context(nc.psum_tensor("ps", [128, 8, 512], F32))[:]
        _, order = build(nc, io, out, sems, mem, None)
        engines, _ = build(nc, io, out, sems, mem, order)
        block = ctx.enter_context(nc.Block())
        sp, pe, dve, act, pool = engines
        block.sync(lambda e: sp.emit(e))
        block.tensor(lambda e: pe.emit(e))
        block.vector(lambda e: dve.emit(e))
        block.scalar(lambda e: act.emit(e))
        block.gpsimd(lambda e: pool.emit(e))


def tables():
    f = np.float32
    p = np.arange(128)
    t = np.arange(T)
    c = {}
    c["ident"] = np.eye(128, dtype=f)
    c["sel"] = (p[:, None] % 32 == 16 * np.arange(2)[None, :]).astype(f)
    c["ones"] = np.ones((128, 128), f)
    c["blk"] = (p[:, None] // 64 == p[None, :] // 64).astype(f)

    def rot(half):
        r = np.zeros((128, 128), f)
        for i in range(128):
            if i % (2 * half) < half:
                r[i + half, i] = -1
            else:
                r[i - half, i] = 1
        return r

    c["rot32"], c["rot128"] = rot(16), rot(64)
    d = p % 64
    freqs = (f(1.0) / (f(10000.0) ** (np.arange(16, dtype=f) / f(16)))).astype(f)
    pos = np.where((d < 32)[:, None], (t // 64)[None, :], (t % 64)[None, :]).astype(f)
    ang = (pos * freqs[d % 16][:, None]).astype(f)
    q = np.arange(128)[:, None, None] + 128 * np.arange(2)[None, :, None]
    amask = np.where(np.abs(q - t[None, None, :]) <= 128, 0.0, NEG).astype(f)
    c["attn_c"] = np.concatenate([np.cos(ang), np.sin(ang), amask.reshape(128, 512)], 1).astype(f)
    inv = (f(1.0) / (f(10000.0) ** np.linspace(0.0, 1.0, 64, dtype=f))).astype(f)
    ang = (t.astype(f)[None, :] * inv[p % 64][:, None]).astype(f)
    c["ret_c"] = np.concatenate([np.cos(ang), np.sin(ang)], 1).astype(f)
    log_g = np.log1p(-(f(2.0) ** (f(-5.0) - np.arange(8, dtype=f)))).astype(f)
    k = p[:, None, None] + 128 * np.arange(2)[None, :, None]
    rel = (t[None, None, :] - k).astype(f)
    c["decay"] = np.stack([np.where(rel >= 0, np.exp(np.maximum(rel, 0) * g), 0).astype(f).reshape(128, 512) for g in log_g])
    parts = []
    for qb in range(2):
        for dil in (1, 4, 16):
            dist = (128 * qb + p)[:, None] - np.arange(128 * (qb + 1))[None, :]
            ok = (dist >= 0) & (dist % dil == 0) & (dist // dil <= 128)
            parts.append(np.where(ok, 0.0, NEG).astype(f))
    c["dil_c"] = np.concatenate(parts, 1)
    i, j = (p % 64)[:, None], np.arange(64)[None, :]
    parts = []
    for back in range(2):
        for n in (1, 2, 4, 8, 16, 32):
            a, b = (i, j) if not back else (j, i)
            parts.append((a // (2 * n) == b // (2 * n)) & (a // n % 2 == 1) & (b // n % 2 == 0))
        a, b = (j, i) if not back else (i, j)
        parts.append((a // 2 == b // 2) & (a % 2 == 1) & (b % 2 == 0))
        parts += [j > i, j >= i] if not back else [j < i, j <= i]
        parts += [i <= j, i < j] if not back else [i >= j, i > j]
    parts.append(i == j)
    c["rwkv_c"] = np.concatenate([x.astype(f) for x in parts], 1)
    return c


def columns(v):
    return np.asarray(v).reshape(-1, 128).T


def tiled(w, width=256):
    k, n = w.shape
    return np.ascontiguousarray(w.reshape(k // 512, 4, 128, n // width, width).transpose(3, 0, 2, 1, 4))


def kernel(**inputs):
    import concourse.bacc as _bacc
    from concourse.bass_utils import run_bass_kernel_spmd as _run

    g = {k: np.asarray(v) for k, v in inputs.items()}
    tab = tables()
    heads = [h for c in range(2) for i in range(4) for h in (8 * c + i, 8 * c + 4 + i)]
    w_in, w_out = g["w_in"][0], g["w_out"][0]
    wq = w_in[:, 0:1024].reshape(2048, 16, 64)[:, heads].reshape(2048, 1024)
    wo = np.concatenate([w_out[0:1024].reshape(16, 64, 2048)[heads].reshape(1024, 2048), w_out[1024:]], 0)
    tsc = []
    for n in ("ts_prev", "ts_next"):
        v = g[n][0]
        tsc.append(np.concatenate([columns(v[0:3328]), v[3328:3456][:, None], v[3360:3488][:, None]], 1))
    cc = np.stack([columns(g["c"][0]), columns(g["c_ctx"])], 2).reshape(128, 32)
    val = dict(sel=tab["sel"], ident=tab["ident"], ones=tab["ones"], blk=tab["blk"], rot32=tab["rot32"], rot128=tab["rot128"], c=cc,
               ada_b=columns(g["ada_b"][0]), norm1=columns(g["norm1_g"][0]), norm2=columns(g["norm2_g"][0]),
               final1=columns(g["final_norm_g"]), norm_a=columns(g["norm_a_2"][0]), norm_b=columns(g["norm_b_2"][0]),
               mem_g=columns(g["mem_norm_g_2"]), kv_g=columns(g["kv_norm_g_2"]), final2=columns(g["final_norm_g_2"]),
               ts=np.concatenate(tsc, 1), a0=np.concatenate([columns(g["a0"][0, d]) for d in range(2)], 1),
               k_k=columns(g["k_k"][0]), k_a=columns(g["k_a"][0]), r_k=columns(g["r_k"][0]), lnx_g=columns(g["lnx_g"][0]),
               lnx_b=columns(g["lnx_b"][0]), sink=np.broadcast_to(g["attn_sink"][0][heads][None, :], (128, 16)))
    fmaj = lambda a: np.ascontiguousarray(a.T.reshape(16, 128, T).transpose(1, 0, 2))
    gd = w_in[:, 4864:5024].reshape(4, 4, 128, 160).transpose(0, 2, 1, 3)
    arrays = dict(
        consts=np.concatenate([val[n] for n in COLS], 1), xT=fmaj(g["x"][0]), ctxT=fmaj(g["ctx"][0]), memT=fmaj(g["mem_2"][0]),
        ada=tiled(g["ada_w"][0]), w_q=tiled(wq), w_ka=tiled(w_in[:, 1024:1280]), w_va=tiled(w_in[:, 1280:1536]),
        w_r=tiled(w_in[:, 1536:2560]), w_k=tiled(w_in[:, 2560:3584]), w_v=tiled(w_in[:, 3584:4608]),
        w_wa=tiled(w_in[:, 4608:4864]), w_gd=gd, w_out=tiled(wo), ffn1=tiled(g["ffn_w1"][0]), ffn3=tiled(g["ffn_w3"][0]),
        ffn2=tiled(g["ffn_w2"][0]), w_in_a=tiled(g["w_in_a_2"][0]), w_out_a=tiled(g["w_out_a_2"][0]),
        w_in_b=tiled(g["w_in_b_2"][0]), w_out_b=tiled(g["w_out_b_2"][0]), mem0=tiled(g["w_mem_kv_2"][0]),
        mem1=tiled(g["w_mem_kv_2"][1]), w_kv=tiled(g["w_kv_2"]), w_up=g["w_up"][0].reshape(128, 1024),
        a_up=g["a_up"][0].reshape(128, 1024), w0=g["w0"][0], g_up=g["g_up"][0], attn_c=tab["attn_c"], ret_c=tab["ret_c"],
        decay=tab["decay"], dil_c=tab["dil_c"], rwkv_c=tab["rwkv_c"])
    nc = _bacc.Bacc("TRN2", target_bir_lowering=False, num_devices=1)
    io, feed = {}, {}
    for name, a in arrays.items():
        a = np.ascontiguousarray(a)
        feed[f"in_{name}"] = a
        io[name] = nc.dram_tensor(f"in_{name}", a.shape, mybir.dt.from_np(a.dtype), kind="ExternalInput").ap()
    io["mem_keep"] = nc.dram_tensor("mem_keep", (2, 8, 128, 512), F32, kind="Internal").ap()
    io["x_keep"] = nc.dram_tensor("x_keep", (128, 16, T), F32, kind="Internal").ap()
    out = nc.dram_tensor("out_0", (128, 16, T), F32, kind="ExternalOutput").ap()
    bass_program(nc, io, out)
    r = _run(nc, [feed], core_ids=[0])
    y = np.asarray(r.results[0]["out_0"])
    return np.ascontiguousarray(y.transpose(2, 1, 0).reshape(1, T, 2048))
```

```python
from contextlib import ExitStack

import numpy as np

import concourse.bass as bass
from concourse import mybir

F32 = mybir.dt.float32
F32R = mybir.dt.float32r
ALU = mybir.AluOpType
ACT = mybir.ActivationFunctionType
AX = mybir.AxisListType
MUL, ADD, SUB, MAX, BYP = ALU.mult, ALU.add, ALU.subtract, ALU.max, ALU.bypass

T = 256
NRAW = 6
NW = 4
AHEAD = 3
NG = 4
NX = 4
NEG = -1e30
DECAY = float(np.exp(-0.5))


def do(method, *args, **kw):
    return lambda: method(*args, **kw)


class Count:

    def __init__(self, sem):
        self.sem, self.n = sem, 0

    def add(self, by):
        self.n += by
        return (self, self.n)


class Engine:

    def __init__(self, nc, sem):
        self.nc, self.count, self.queue, self.seen = nc, Count(sem), [], {}

    def waits(self, deps):
        need = {}
        for d in flat(deps):
            if d[1] > max(self.seen.get(d[0], 0), need.get(d[0], 0)):
                need[d[0]] = d[1]
        self.seen.update(need)
        return [(c.sem, v) for c, v in need.items()]

    def __call__(self, fn, *deps, inc=True):
        token = self.count.add(1) if inc else None
        self.queue.append((self.waits(deps), fn, self.count.sem if inc else None, 1))
        return token

    def dma(self, out, in_, count, *deps):
        token = count.add(16)
        self.queue.append((self.waits(deps), do(self.nc.dma_start, out, in_), count.sem, 16))
        return token

    def last(self):
        return (self.count, self.count.n) if self.count.n else None

    def emit(self, e):
        for waits, fn, sem, by in self.queue:
            for s, v in waits:
                e.wait_ge(s, v)
            if fn is not None:
                ins = fn()
                if sem is not None:
                    ins.then_inc(sem, by)


def flat(deps):
    for d in deps:
        if isinstance(d, list):
            yield from flat(d)
        elif d is not None:
            yield d


class Pool:

    def __init__(self, views):
        self.views, self.free = views, [(i, []) for i in range(len(views))]

    def get(self):
        i, deps = self.free.pop(0)
        return Buf(self, i, self.views[i], deps)


class Buf:
    def __init__(self, pool, i, ap, deps):
        self.pool, self.i, self.ap, self.deps, self.tok = pool, i, ap, deps, []

    def done(self, *tokens):
        self.pool.free.append((self.i, list(flat(tokens))))


class Acts:

    def __init__(self, hi, lo):
        self.hi, self.lo = hi, lo
        self.tok = [[] for _ in range(hi.shape[1])]


def run_all(*gens):
    live = list(gens)
    while live:
        for g in list(live):
            for _ in range(g[1]):
                if next(g[0], "end") == "end":
                    live.remove(g)
                    break


def rolling(gens, width):
    live = []
    while live or gens:
        if gens and len(live) < width:
            live.append(gens.pop(0))
        for g in list(live):
            if next(g, "end") == "end":
                live.remove(g)


def rest(g):
    for _ in g:
        pass


def build(nc, io, out, sems, mem, order):
    SP, PE, DVE, AC, PO = (Engine(e, sems[f"e{i}"]) for i, e in enumerate((nc.sync, nc.tensor, nc.vector, nc.scalar, nc.gpsimd)))
    engines = (SP, PE, DVE, AC, PO)
    new_sem = iter(range(100))

    def counter():
        return Count(sems[f"d{next(new_sem)}"])

    def fence():
        return [e.last() for e in engines]

    A = mem.__getitem__
    ps = A("ps")

    raw_sem = [counter() for _ in range(NRAW)]
    rec = []
    slots = {}
    gate = dict(at=0 if order is None else next(i for i, k in enumerate(order) if k[0] == "w_out"), deps=[])
    st = dict(i=0, split=0, dma=0, nsplit=0)
    released = {}
    wdone = {}

    def emit_dma(j):
        name, nt, kg, w, split = order[j]
        src = io[name][nt, kg] if split != "tail" else io[name][kg]
        dst = A("raw")[:, j % NRAW, 0:4 * w]
        slots[j] = dict(raw=dst.rearrange("p (c n) -> p c n", c=4), w=w,
                        tok=SP.dma(dst, src.rearrange("p c n -> p (c n)"), raw_sem[j % NRAW],
                                   released.get(j - NRAW)))
        st["dma"] += 1

    def emit_split(j):
        s = slots[j]
        w = s["w"]
        if order[j][4] == "raw":
            return
        n = st["nsplit"]
        st["nsplit"] += 1
        s["n"] = n
        src = A("raw")[:, j % NRAW, 0:4 * w]
        hi, lo = A("wh")[:, n % NW, 0:4 * w], A("wl")[:, n % NW, 0:4 * w]
        t1 = AC(do(nc.scalar.activation, hi, src, ACT.Copy), s["tok"], wdone.get(n - NW), gate["deps"])
        eng = DVE if n % 2 else PO
        t2 = eng(do(eng.nc.tensor_tensor, lo, src, hi.bitcast(F32), SUB), s["tok"], t1, wdone.get(n - NW), gate["deps"])
        s["hi"], s["lo"] = (v.rearrange("p (c n) -> p c n", c=4) for v in (hi, lo))
        s["ready"] = [t1, t2]
        released[j] = [t1, t2]

    def split_ahead(i=None):
        for j in range(st["split"], min((st["i"] if i is None else i) + AHEAD + 1, gate["at"])):
            while st["dma"] <= j:
                emit_dma(st["dma"])
            emit_split(j)
            st["split"] = j + 1

    def next_slot(key):
        i = st["i"]
        st["i"] += 1
        if order is None:
            rec.append(key)
            w = key[3]
            hi = A("wh")[:, 0, 0:4 * w].rearrange("p (c n) -> p c n", c=4)
            return i, dict(raw=A("raw")[:, 0, 0:4 * w].rearrange("p (c n) -> p c n", c=4), hi=hi, lo=hi,
                           ready=[], tok=None, n=0)
        assert order[i] == key
        split_ahead(i)
        while st["dma"] < len(order) and (st["dma"] < NRAW or st["dma"] - NRAW in released):
            emit_dma(st["dma"])
        return i, slots[i]

    def open_gate(deps):
        if order is not None:
            gate.update(at=len(order), deps=deps)

    def slot_done(i, s, token):
        if order is None:
            return
        if order[i][4] == "raw":
            released[i] = [token]
        else:
            wdone[s["n"]] = token

    G = Pool([ps[:, b, :] for b in range(NG)])
    X = Pool([ps[:, NG + b, :] for b in range(NX)])

    def two(pool):
        ids = {i: k for k, (i, _) in enumerate(pool.free)}
        for i in sorted((0, 2), key=lambda i: max(ids.get(i, 9), ids.get(i + 1, 9))):
            if i in ids and i + 1 in ids:
                parts = [f for f in pool.free if f[0] in (i, i + 1)]
                pool.free = [f for f in pool.free if f[0] not in (i, i + 1)]
                return Two(pool, i, [d for _, d in parts])
        raise RuntimeError("no two banks")

    class Two:
        def __init__(self, pool, i, deps):
            self.pool, self.i, self.deps = pool, i, deps
            base = NG + i if pool is X else i
            self.ap = ps[:, base:base + 2, :].rearrange("p b n -> p (b n)")

        def done(self, *tokens):
            for k in (self.i, self.i + 1):
                self.pool.free.append((k, list(flat(tokens))))

    def gemm(name, nt, kgs, outs, nb, evac, w=256, split=True, deps=None, kbase=0):
        banks = [G.get() for _ in range(nb)]
        begun = set()
        for at, kg in enumerate(kgs):
            i, s = next_slot((name, nt, kg, w, split))
            wait = [s["ready"], deps] if deps else s["ready"]
            hi, lo = s["hi"], s["lo"]
            for kc in range(4):
                k = (kg - kbase) * 4 + kc
                for n, (b, off, kind, c0, acts, tb) in enumerate(outs):
                    ah, al = acts.hi[:, k, :], acts.lo[:, k, :]
                    if kind == "B":
                        o = banks[b].ap[:, off:off + T]
                        pairs = [(hi[:, kc, c0:c0 + 128], ah), (hi[:, kc, c0:c0 + 128], al),
                                 (lo[:, kc, c0:c0 + 128], ah)]
                    else:
                        o = banks[b].ap[:, off:off + w]
                        r = slice(128 * tb, 128 * tb + 128)
                        pairs = [(ah[:, r], hi[:, kc, :]), (ah[:, r], lo[:, kc, :]), (al[:, r], hi[:, kc, :])]
                    for m, (x, y) in enumerate(pairs):
                        first = b not in begun
                        begun.add(b)
                        end = kc == 3 and n == len(outs) - 1 and m == 2
                        last = at == len(kgs) - 1 and kc == 3 and m == 2
                        tok = PE(do(nc.tensor.matmul, o, x, y, start=first, stop=last, skip_group_check=True),
                                 wait, acts.tok[k], banks[b].deps if first else None, inc=end)
                        wait = None
            slot_done(i, s, tok)
            yield
        evac(banks, tok)

    cs = A("const")

    def cst(name, n):
        o = COLS[name]
        return cs[:, o:o + n]

    c_load = counter()
    const_tok = SP.dma(cs[:, 0:NCONST], io["consts"], c_load)
    ident, ones, blk = cst("ident", 128), cst("ones", 128), cst("blk", 128)

    tmps = Pool([A("tm")[:, i, :] for i in range(4)])
    rsts = Pool([A("rst")[:, i, :] for i in range(2)])
    xt = A("x")

    def rms(src, nch, deps, sq, eps=1e-6, by=None):
        bank = X.get()
        for q in range(nch // 4):
            b = sq.get()
            t = AC(do(nc.scalar.activation, b.ap, src[:, 4 * q:4 * q + 4, :], ACT.Square), deps, b.deps,
                   [by[c] for c in range(4 * q, 4 * q + 4)] if by else None)
            for c in range(4):
                m = PE(do(nc.tensor.matmul, bank.ap[:, 0:T], ones, b.ap[:, c, :],
                                                         start=(q == 0 and c == 0), stop=(q == nch // 4 - 1 and c == 3)),
                       t, const_tok, bank.deps, inc=(c == 3))
            b.done(m)
        return inverse_root(bank, m, nch, eps)

    def inverse_root(bank, m, nch, eps=1e-6):
        r = rsts.get()
        d1 = DVE(do(nc.vector.tensor_scalar, r.ap, bank.ap[:, 0:T], 1.0 / (128 * nch), eps, MUL, ADD), m, r.deps)
        bank.done(d1)
        d2 = AC(do(nc.scalar.activation, r.ap, r.ap, ACT.Sqrt), d1)
        r.tok = DVE(do(nc.vector.reciprocal, r.ap, r.ap), d2)
        return r

    def split(dst, c, n, src, *deps, eng=PO):
        hi, lo = dst.hi[:, c:c + n, :], dst.lo[:, c:c + n, :]
        t1 = AC(do(nc.scalar.activation, hi, src, ACT.Copy), *deps)
        t2 = eng(do(eng.nc.tensor_tensor, lo, src, hi.bitcast(F32), SUB), t1, *deps)
        for k in range(c, c + n):
            dst.tok[k] = [t1, t2]
        return [t1, t2]

    def normed(*args):
        rest(normed_steps(*args))

    def normed_steps(src, r, gain, shift, dst, deps, last=True):
        for c in range(16):
            b = tmps.get()
            t = DVE(do(nc.vector.scalar_tensor_tensor, b.ap, src[:, c, :], gain[:, c:c + 1], r.ap, MUL, MUL),
                    r.tok, b.deps, deps)
            hi, lo = dst.hi[:, c, :], dst.lo[:, c, :]
            if shift is None:
                b.done(split(dst, c, 1, b.ap.rearrange("p (o n) -> p o n", o=1), t, deps, eng=(DVE, PO)[c % 2]))
            else:
                t1 = AC(do(nc.scalar.activation, hi, b.ap, ACT.Identity, bias=shift[:, c:c + 1]), t, deps)
                t2 = DVE(do(nc.vector.scalar_tensor_tensor, lo, b.ap, shift[:, c:c + 1], hi.bitcast(F32), ADD, SUB), t1)
                dst.tok[c] = [t1, t2]
                b.done(t1, t2)
            yield
        if last:
            r.done(t)

    def tanh_half(dst, src, *deps):
        return AC(do(nc.scalar.activation, dst, src, ACT.Tanh, scale=0.5), *deps)

    HA, HB = Acts(A("hah"), A("hal")), Acts(A("hbh"), A("hbl"))
    mix = A("mix")
    work4 = Pool([A("work")[:, 1024 * i:1024 * i + 1024].rearrange("p (c n) -> p c n", c=4) for i in range(7)])

    m32, l_m, l_c, l_x = A("hal32").rearrange("p (c n) -> p c n", c=16), counter(), counter(), counter()
    m_tok = SP.dma(m32, io["memT"], l_m)
    c_tok = SP.dma(mix[:, 0:16, :], io["ctxT"], l_c)
    x_tok = SP.dma(xt, io["xT"], l_x)
    sc = A("sc")
    th = tmps.get()
    cv = cst("c", 32)
    t = tanh_half(th.ap[:, 0:32], cv, const_tok)
    t = DVE(do(nc.vector.scalar_tensor_tensor, sc, th.ap[:, 0:32], 1.0, cv, ADD, MUL), t)
    sc_tok = DVE(do(nc.vector.tensor_scalar, sc, sc, 0.5, None, MUL), t)
    th.done(sc_tok)
    sc16 = A("sc16")
    sc_tok = DVE(do(nc.vector.tensor_copy, sc16.rearrange("p (k n) -> p k n", n=16), sc.unsqueeze(2).to_broadcast([128, 32, 16])), sc_tok)
    mod = A("mod")
    ada_b, sel = cst("ada_b", 96), cst("sel", 2)
    mod_tok = {}

    ada_late = []

    def ada(nt):
        bank = G.get()
        for kg in range(4):
            i, s = next_slot(("ada", nt, kg, 256, "raw"))
            for g in range(4):
                k = 4 * kg + g
                w = sc16[:, 32 * k:32 * k + 32]
                tok = PE(do(nc.tensor.matmul, bank.ap[32 * g:32 * g + 32, 0:256], w, s["raw"][:, g, :], start=(kg == 0),
                            stop=(kg == 3), skip_group_check=True),
                         s["tok"], sc_tok, bank.deps if kg == 0 else None, inc=(g == 3))
            slot_done(i, s, tok)
            if kg == 1:
                ada_end()
            yield
        part = tmps.get()
        t = AC(do(nc.scalar.activation, part.ap, bank.ap[:, 0:256], ACT.Copy), tok, part.deps)
        ada_late.append((nt, bank, part, t))

    def ada_end():
        if not ada_late:
            return
        nt, bank, part, t = ada_late.pop()
        for fb in range(2):
            tok = PE(do(nc.tensor.matmul, bank.ap[:, 256 + 2 * fb:258 + 2 * fb], part.ap[:, 128 * fb:128 * fb + 128], sel,
                        start=True, stop=True, skip_group_check=True), t, const_tok, inc=(fb == 1))
        part.done(tok)
        dst = mod[:, 4 * nt:4 * nt + 4].rearrange("p (f t) -> p f t", t=2)
        src = bank.ap[:, 256:260].rearrange("p (f t) -> p f t", t=2)
        b = ada_b[:, 2 * nt:2 * nt + 2].unsqueeze(2).to_broadcast([128, 2, 2])
        mod_tok[nt] = DVE(do(nc.vector.tensor_tensor, dst, src, b, ADD), tok, const_tok)
        bank.done(mod_tok[nt])

    sq4 = Pool(work4.views[0:4])
    wsp = A("work")
    spill = Pool([wsp[:, 4096 + 512 * i:4608 + 512 * i] for i in range(6)])
    s_mem = [counter() for _ in range(6)]
    mem_saved = {}

    def memory_kv():
        for lay in range(2):
            for n in range(8):
                def ev(banks, tok):
                    b = spill.get()
                    t = AC(do(nc.scalar.activation, b.ap, banks[0].ap, ACT.Copy), tok, b.deps)
                    banks[0].done(t)
                    mem_saved[lay, n] = PO.dma(io["mem_keep"][lay, n], b.ap, s_mem[b.i], t)
                    b.done(mem_saved[lay, n])
                outs = [(0, 256 * i, "B", 128 * i, HB, 0) if n < 4 else (0, 256 * i, "A", 0, HB, i) for i in range(2)]
                yield from gemm(f"mem{lay}", n, range(4), outs, 1, ev)

    rm = rms(m32, 16, m_tok, sq4)
    normed(m32, rm, cst("mem_g", 16), None, HB, [const_tok])
    rc = rms(mix, 16, c_tok, sq4)
    rx = rms(xt, 16, x_tok, sq4)

    def ada_first():
        for nt in range(16):
            yield from ada(nt)
        ada_end()

    run_all((ada_first(), 1), (memory_kv(), 1))
    f_mem = fence()
    mods = mod.rearrange("p (s c t) -> p s t c", s=6, t=2)

    def plus_one(dst, gain, scale, *deps):
        return DVE(do(nc.vector.scalar_tensor_tensor, dst, scale, 1.0, gain, ADD, MUL), *deps)

    gs = A("gs")
    g1x = plus_one(gs[:, 0:16], cst("norm1", 16), mods[:, 1, 0, :], mod_tok[15], const_tok)
    g1c = plus_one(gs[:, 16:32], cst("norm1", 16), mods[:, 1, 1, :], mod_tok[15], const_tok)
    normed(mix, rc, gs[:, 16:32], mods[:, 0, 1, :], HB, [g1c, mod_tok[7], f_mem])
    normed(xt, rx, gs[:, 0:16], mods[:, 0, 0, :], HA, [g1x, mod_tok[7], f_mem])

    ph = counter()
    phc = A("phc")
    cosr, sinr, amask = phc[:, 0:256], phc[:, 256:512], phc[:, 512:1024].rearrange("p (q n) -> p q n", q=2)
    ph_tok = SP.dma(phc[:, 0:1024], io["attn_c"], ph)
    wk = A("work")
    vT = wk[:, 0:4096].rearrange("p (c n) -> p c n", c=8)
    kA = wk[:, 4096:5120].rearrange("p (c n) -> p c n", c=2)
    vA = wk[:, 5120:6144].rearrange("p (b n) -> p b n", b=4)
    wdad = wk[:, 6144:7168].rearrange("p (c n) -> p c n", c=2)
    gd = wk[:, 7168:7680].rearrange("p (c n) -> p c n", c=2)
    kT = A("xk")
    qT, rT = A("hb_q"), A("hb_r")
    after_norm = [fence(), list(mem_saved.values())]
    ts = cst("ts", 56)
    ts_rem = A("tsr")
    t = DVE(do(nc.vector.tensor_tensor, ts_rem, ts[:, 0:28], ts[:, 28:56], ADD), const_tok)
    tsr_tok = DVE(do(nc.vector.tensor_scalar, ts_rem, ts_rem, -1.0, 1.0, MUL, ADD), t)

    def shift_self(dst, src, f, *deps):
        return AC(do(nc.scalar.activation, dst, src, ACT.Copy, scale=ts_rem[:, f:f + 1]), tsr_tok, *deps)

    def shifted(dst, src, f, nseq, t):
        d3, s3 = (v.rearrange("p (q n) -> p q n", q=nseq) for v in (dst, src))
        t = DVE(do(nc.vector.scalar_tensor_tensor, d3[:, :, 1:T], s3[:, :, 0:T - 1], ts[:, f:f + 1], d3[:, :, 1:T],
                                                 MUL, ADD), t)
        return DVE(do(nc.vector.scalar_tensor_tensor, d3[:, :, 0:T - 1], s3[:, :, 1:T], ts[:, 28 + f:29 + f],
                                                    d3[:, :, 0:T - 1], MUL, ADD), t)

    both = [(fb, 256 * a, "B", 128 * fb, (HB, HA)[a], 0) for fb in range(2) for a in range(2)]
    xonly = [(0, 256 * fb, "B", 128 * fb, HA, 0) for fb in range(2)]
    ztok = {}
    dead = [after_norm]

    def ev_shift2(dst, f0, key):
        def ev(banks, tok):
            for fb in range(2):
                t = shift_self(dst(fb), banks[fb].ap, f0 + fb, tok, dead)
                t = shifted(dst(fb), banks[fb].ap, f0 + fb, 2, t)
                banks[fb].done(t)
                ztok[key, fb] = t
        return ev

    for n in range(4):
        rest(gemm("w_k", n, range(4), both, 2, ev_shift2(lambda fb, n=n: kT[:, 2 * n + fb, :], 8 + 2 * n, ("k", n))))
    for n in range(4):
        rest(gemm("w_v", n, range(4), both, 2, ev_shift2(lambda fb, n=n: vT[:, 2 * n + fb, :], 16 + 2 * n, ("v", n))))
    rest(gemm("w_wa", 0, range(4), both, 2, ev_shift2(lambda fb: wdad[:, fb, :], 24, "wa")))

    def rope(dst, bank, off, w, scale, tok, rot, cos, sin, ctok):
        raw = tmps.get()
        t1 = AC(do(nc.scalar.activation, raw.ap, bank.ap[:, off:off + w], ACT.Copy, scale=scale), tok, raw.deps)
        b = X.get()
        t2 = PE(do(nc.tensor.matmul, b.ap[:, 0:w], rot, raw.ap, start=True, stop=True), t1, const_tok, b.deps)
        t3 = PO(do(nc.gpsimd.tensor_tensor, dst, raw.ap, cos, MUL), t1, ctok, dead)
        t4 = DVE(do(nc.vector.tensor_tensor, raw.ap, b.ap[:, 0:w], sin, MUL), t2, t3, ctok)
        b.done(t4)
        t5 = DVE(do(nc.vector.tensor_tensor, dst, dst, raw.ap, ADD), t4)
        raw.done(t5)
        return t1, t5

    def ev_kA(banks, tok):
        for fb in range(2):
            t0 = AC(do(nc.scalar.activation, kA[:, fb, 256:512], banks[fb].ap[:, 0:256], ACT.Copy), tok, dead)
            t1, t2 = rope(kA[:, fb, 0:256], banks[fb], 256, 256, 1.0, tok, cst("rot32", 128), cosr, sinr, ph_tok)
            banks[fb].done(t0, t1)
            ztok["kA", fb] = [t0, t2]

    rest(gemm("w_ka", 0, range(4), both, 2, ev_kA))

    def ev_vA(banks, tok):
        for b in range(2):
            t = AC(do(nc.scalar.activation, vA[:, 2 * b:2 * b + 2, :], banks[b].ap.rearrange("p (o n) -> p o n", o=2),
                                               ACT.Copy), tok, dead)
            banks[b].done(t)
            ztok["vA", b] = t

    rest(gemm("w_va", 0, range(4), [(a, 256 * tb, "A", 0, (HA, HB)[a], tb) for a in range(2) for tb in range(2)], 2, ev_vA))
    hb_free = fence()

    def ev_r(n):
        def ev(banks, tok):
            own = [shift_self(rT[:, 2 * n + fb, :], banks[0].ap[:, 256 * fb:256 * fb + 256], 2 * n + fb, tok, hb_free)
                   for fb in range(2)]
            for fb in range(2):
                t = shifted(rT[:, 2 * n + fb, :], banks[0].ap[:, 256 * fb:256 * fb + 256], 2 * n + fb, 1, own)
                ztok["r", 2 * n + fb] = t
            banks[0].done(t)
        return ev

    def ev_q(n):
        def ev(banks, tok):
            dead.append(hb_free)
            ts_ = []
            for fb in range(2):
                t1, t2 = rope(qT[:, 2 * n + fb, :], banks[0], 256 * fb, 256, 0.125, tok, cst("rot32", 128), cosr, sinr, ph_tok)
                ts_.append(t1)
                ztok["q", 2 * n + fb] = t2
            banks[0].done(ts_)
        return ev

    def ev_gd(banks, tok):
        own = [shift_self(gd[:, fb, :], banks[0].ap[:, 256 * fb:256 * fb + 256], 26 + fb, tok, dead) for fb in range(2)]
        out_ = []
        for fb in range(2):
            t = shifted(gd[:, fb, :], banks[0].ap[:, 256 * fb:256 * fb + 256], 26 + fb, 1, own)
            out_.append(t)
            t = tanh_half(gd[:, fb, :], gd[:, fb, :], t)
            ztok["gd", fb] = DVE(do(nc.vector.tensor_scalar, gd[:, fb, :], gd[:, fb, :], 0.5, 0.5, MUL, ADD), t)
        banks[0].done(out_)

    for n in range(4):
        rest(gemm("w_q", n, range(4), xonly, 1, ev_q(n)))

    al = A("hbl32")
    pbuf = Pool([al[:, 512 * i:512 * i + 512] for i in range(3)])
    ptbuf = Pool([al[:, 1536 + 512 * i:2048 + 512 * i].rearrange("p (b n) -> p b n", b=4) for i in range(3)])
    cols = A("cols")
    sink = cst("sink", 16)

    def attn():
        out_bank = {}

        def scores(n):
            c, rem = divmod(n, 4)
            half, qb = divmod(rem, 2)
            r = slice(64 * half, 64 * half + 64)
            b = X.get()
            t = PE(do(nc.tensor.matmul, b.ap, qT[r, c, 128 * qb:128 * qb + 128], kA[r, c // 4, :], start=True, stop=True),
                   ztok["q", c], ztok["kA", c // 4], b.deps)
            p = pbuf.get()
            k = 8 * (n % 8)
            mx, nm = (cols[:, k + i:k + i + 1] for i in range(2))
            sk = sink[:, 2 * c + half:2 * c + half + 1]
            t0 = AC(do(nc.scalar.activation, p.ap[:, 256:512], b.ap[:, 256:512], ACT.Copy), t, p.deps, hb_free)
            t1 = DVE(do(nc.vector.tensor_tensor, p.ap[:, 0:256], b.ap[:, 0:256], amask[:, qb, :], ADD), t0, p.deps, ph_tok, hb_free)
            b.done(t0, t1)
            t2 = DVE(do(nc.vector.tensor_reduce, mx, p.ap, AX.X, MAX), t0, t1)
            p.tok = DVE(do(nc.vector.tensor_scalar, nm, mx, sk, -1.0, MAX, MUL), t2)
            return p

        def soft(n, p):
            c, rem = divmod(n, 4)
            half, qb = divmod(rem, 2)
            k = 8 * (n % 8)
            nm, rs, es = (cols[:, k + i:k + i + 1] for i in range(1, 4))
            sk = sink[:, 2 * c + half:2 * c + half + 1]
            t3 = p.tok
            t4 = AC(do(nc.scalar.activation, p.ap, p.ap, ACT.Exp, bias=nm, accum_out=rs), t3)
            t5 = AC(do(nc.scalar.activation, es, sk, ACT.Exp, bias=nm), t3)
            t6 = DVE(do(nc.vector.tensor_tensor, rs, rs, es, ADD), t4, t5)
            t7 = DVE(do(nc.vector.reciprocal, rs, rs), t6)
            p.tok = DVE(do(nc.vector.tensor_scalar, p.ap, p.ap, rs, None, MUL), t7)

        def apply(n, p, between):
            c, rem = divmod(n, 4)
            half, qb = divmod(rem, 2)
            kv = 2 * (c // 4) + half
            b = X.get()
            for k in range(4):
                t = PE(do(nc.tensor.transpose, b.ap[:, 128 * k:128 * k + 128], p.ap[:, 128 * k:128 * k + 128], ident),
                       p.tok, b.deps, inc=(k == 3))
            p.done(t)
            pt = ptbuf.get()
            t1 = AC(do(nc.scalar.activation, pt.ap, b.ap.rearrange("p (b n) -> p b n", b=4), ACT.Copy), t, pt.deps, hb_free)
            b.done(t1)
            between()
            yield
            if rem == 0:
                out_bank[c] = X.get()
            o = out_bank[c]
            for k in range(4):
                t = PE(do(nc.tensor.matmul, o.ap[64 * half:64 * half + 64, 128 * qb:128 * qb + 128],
                                               vA[:, k, 64 * kv:64 * kv + 64], pt.ap[:, k, :], start=(k == 0), stop=(k == 3)),
                       t1, ztok["vA", 0], ztok["vA", 1], o.deps, inc=(k == 3))
            pt.done(t)
            if rem == 3:
                t = AC(do(nc.scalar.activation, mix[:, c, :], o.ap[:, 0:256], ACT.Copy), t, after_norm)
                o.done(t)

        ps_ = {0: scores(0), 1: scores(1)}
        soft(0, ps_[0])
        yield
        for n in range(32):
            def between():
                if n + 2 < 32:
                    ps_[n + 2] = scores(n + 2)
                if n + 1 < 32:
                    soft(n + 1, ps_[n + 1])
            yield from apply(n, ps_.pop(n), between)
            yield

    def ada_rest():
        for nt in range(16, 48):
            yield from ada(nt)

    filler = ada_rest()

    def limited(g, n):
        for _ in range(n):
            if next(g, "end") == "end":
                return
            yield

    def chain(*gens):
        for g in gens:
            yield from g

    def r_and_gd():
        for n in range(4):
            yield from gemm("w_r", n, range(4), xonly, 1, ev_r(n))
        yield from gemm("w_gd", 0, range(4), [(0, 256 * fb, "B", 32 * fb, HA, 0) for fb in range(2)], 1, ev_gd, w=160,
                        split="tail")

    run_all((attn(), 2), (chain(r_and_gd(), limited(filler, 14)), 1))

    f0 = fence()
    rl = counter()
    rwc = A("rwc")
    mix_saved = PO.dma(io["mix_keep"], mix[:, 0:8, :], counter(), f0)
    AC.dma(rwc, io["rwkv_c"], rl, f0)
    wup, aup, w0r = A("wup"), A("aup"), A("w0r")
    AC.dma(wup, io["w_up"], rl, f0)
    AC.dma(aup, io["a_up"], rl, f0)
    rl_tok = AC.dma(w0r, io["w0"], rl, f0)
    tmps.free = [f for f in tmps.free if f[0] > 1]
    kk = A("kk")
    kkc, kac, rkc = cst("k_k", 8), cst("k_a", 8), cst("r_k", 8)
    a0c = cst("a0", 16)
    i64 = rwc[:, 1408:1472]

    def fc(ap):
        return ap.rearrange("p (c n) -> p c n", c=8)

    lwb, Pex, Pin, Pinv, ab, tb_, kd, bh, kh = (A(n) for n in ("lw", "Pex", "Pin", "Pinv", "ab", "tb", "kd", "bh", "kh"))
    sets = [{n: A(n + p) for n in ("ar", "BTr", "AKA", "X", "btok", "ktok", "vtok")} for p in "01"]
    for p in range(2):
        sets[p]["BT"], sets[p]["Xt"] = [A(f"BTa{p}"), A(f"BTb{p}")], [A(f"Xta{p}"), A(f"Xtb{p}")]
    T1, R, U, Zs, pcs = A("T1"), A("R"), A("U"), [A("Z0"), A("Z1")], [cols[:, 8 * d:8 * d + 8] for d in range(2)]
    yT = mix[:, 8:16, :]

    def bc(ap, n, m):
        return ap.unsqueeze(1).to_broadcast([128, n, m])

    def bcol(ap, n, m):
        return ap.unsqueeze(2).to_broadcast([128, n, m])

    lora = (wdad, A("pad"))
    t = AC(do(nc.scalar.activation, wdad[:, 0, :], wdad[:, 0, :], ACT.Tanh), ztok["wa", 0], f0)
    t = [AC(do(nc.scalar.activation, lora[1][64:128, :, :], wdad[64:128, :, :], ACT.Copy), t, ztok["wa", 1]),
         DVE(do(nc.vector.memset, lora[1][0:64, :, :], 0.0), f0)]
    wd_tok = [t, DVE(do(nc.vector.memset, wdad[64:128, :, :], 0.0), t)]
    hk, hc, a0h = cols[:, 16:24], cols[:, 24:32], cols[:, 32:48]
    DVE(do(nc.vector.tensor_scalar, hk, kac, 0.5, None, MUL), f0)
    DVE(do(nc.vector.tensor_scalar, hc, kac, -1.0, 2.0, MUL, ADD), f0)
    DVE(do(nc.vector.tensor_scalar, a0h, a0c, 0.5, None, MUL), f0)
    norm2 = A("nk")
    sqs = Pool([A(n + "0") for n in ("btok", "ktok", "vtok", "X")])
    ks = [DVE(do(nc.vector.tensor_scalar, kk[:, c, :], kT[:, c, :], kkc[:, c:c + 1], None, MUL), ztok[("k", c // 2), c % 2],
              f0, const_tok) for c in range(8)]
    for c in range(8):
        sq = sqs.get()
        t = AC(do(nc.scalar.activation, sq.ap, kk[:, c, :], ACT.Square), ks[c], sq.deps, f0)
        b = X.get()
        t = PE(do(nc.tensor.matmul, b.ap, blk, sq.ap, start=True, stop=True), t, b.deps)
        sq.done(t)
        ks[c] = DVE(do(nc.vector.tensor_scalar, norm2[:, c, :], b.ap, 1e-12, None, MAX), t)
        b.done(ks[c])
    kk_tok = []
    for c, eng in ((0, DVE), (4, PO)):
        q4 = slice(c, c + 4)
        t = AC(do(nc.scalar.activation, norm2[:, q4, :], norm2[:, q4, :], ACT.Sqrt), ks[c:c + 4])
        t = DVE(do(nc.vector.reciprocal, norm2[:, q4, :], norm2[:, q4, :]), t)
        kk_tok.append(eng(do(eng.nc.tensor_tensor, kk[:, q4, :], kk[:, q4, :], norm2[:, q4, :], MUL), t))

    its = [(d, n) for n in range(8) for d in range(2)]
    free = {}
    done = [[], []]
    state, z_tok, u_read, r_read, t1_read = {}, [None, None], [], [], []
    y_tok = {}
    for q in sets:
        for h, (x, y) in enumerate(zip(q["BT"], q["Xt"])):
            o = slice(64 - 64 * h, 128 - 64 * h)
            DVE(do(nc.vector.memset, x[o, :], 0.0), kk_tok, mix_saved)
            DVE(do(nc.vector.memset, y[o, :], 0.0), kk_tok)
    fr = fence()

    def dense(out, *deps, at=0):
        PE(do(nc.tensor.matmul, out[:, at:at + 256], ident, cs[:, 0:256], start=True, stop=True), *deps, inc=False)

    def heads(out, fn, *deps, at=(0, 4)):
        for c in range(8):
            if c in at:
                dense(out, *deps, at=c * out.shape[1] // 8)
            for hh in range(2):
                t = PE(fn(slice(64 * hh, 64 * hh + 64), c), *deps, inc=(c == 7 and hh == 1))
        return t

    def prepare(i):
        d, n = its[i]
        q = sets[i % 2]
        ck = n if d == 0 else (3 - n if n < 4 else 11 - n)
        lat = ck >= 4
        o = 704 * d
        pair, tri = rwc[:, o + 448:o + 576], rwc[64 * d:64 * d + 64, o + 576:o + 704]
        h, tk, tx = slice(64 * d, 64 * d + 64), slice(64 * ck, 64 * ck + 64), slice(64 * (ck - 4), 64 * (ck - 4) + 64)
        b2 = two(G)
        for j in range(2):
            t = PE(do(nc.tensor.matmul, b2.ap[h, 512 * j:512 * j + 512], lora[d][:, 0, tk], wup[:, 512 * j:512 * j + 512],
                      start=True, stop=True), wd_tok, rl_tok, b2.deps, inc=(j == 1))
        lw = lwb[h, :]
        t = DVE(do(nc.vector.tensor_tensor, lw, b2.ap[h, :], w0r[h, :], ADD), t, free.get(("lw", d)), rl_tok, fr)
        b2.done(t)
        t = tanh_half(lw, lw, t)
        lw_tok = DVE(do(nc.vector.tensor_scalar, lw, lw, 1.0, -0.5 * DECAY, ADD, MUL), t)
        yield
        ba = G.get()
        for c in range(8):
            t = PE(do(nc.tensor.matmul, ba.ap[:, 64 * c:64 * c + 64], aup[:, 128 * c:128 * c + 128], lora[d][:, 1, tk],
                      start=True, stop=True), wd_tok, rl_tok, ba.deps, inc=(c == 7))
        t = DVE(do(nc.vector.tensor_tensor, fc(ab), fc(ba.ap), bcol(a0c[:, 8 * d:8 * d + 8], 8, 64), ADD), t, free.get("ab"), fr)
        ba.done(t)
        t = tanh_half(ab, ab, t)
        a_tok = DVE(do(nc.vector.tensor_scalar, ab, ab, 0.5, 0.5, MUL, ADD), t)
        yield
        b2 = two(G)
        for c in range(8):
            t = PE(do(nc.tensor.matmul, b2.ap[:, 128 * c:128 * c + 128], lw[:, 128 * c:128 * c + 128], tri,
                      start=True, stop=True), lw_tok, b2.deps, inc=(c == 7))
        free["lw", d] = [t]
        L = b2.ap.rearrange("p (c n) -> p c n", c=8)
        t3 = AC(do(nc.scalar.activation, fc(Pinv), L[:, :, 0:64], ACT.Exp, scale=-1.0), t, free.get("Pinv"), fr)
        t2 = AC(do(nc.scalar.activation, fc(Pex), L[:, :, 64:128], ACT.Exp), t, free.get("Pex"), fr)
        t1 = AC(do(nc.scalar.activation, fc(Pin), L[:, :, 0:64], ACT.Exp), t, free.get("Pin"), fr)
        b2.done(t1)
        kv, kkv = kT[:, :, tk], kk[:, :, tk]
        u = DVE(do(nc.vector.scalar_tensor_tensor, fc(tb_), fc(ab), -1.0, bcol(kac, 8, 64), ADD, MUL), a_tok, free.get("tb"), fr)
        kd_tok = DVE(do(nc.vector.scalar_tensor_tensor, fc(kd), fc(tb_), 1.0, kv, ADD, MUL), u, free.get("kd"), fr)
        u = PO(do(nc.gpsimd.tensor_tensor, fc(tb_), kkv, fc(ab), MUL), a_tok, kd_tok, kk_tok)
        free["ab"] = [u]
        yield
        old = [done[i % 2], fr]
        bv = G.get()
        t = heads(bv.ap, lambda s, c: do(nc.tensor.matmul, bv.ap[s, 64 * c:64 * c + 64], vT[:, c, tk], ident[:, s], start=True, stop=True),
                  bv.deps, [ztok[("v", c // 2), c % 2] for c in range(8)], at=())
        vt_tok = AC(do(nc.scalar.activation, q["vtok"], bv.ap, ACT.Copy), t, old)
        bv.done(vt_tok)
        yield
        kh_tok = DVE(do(nc.vector.tensor_tensor, kh, kd, Pinv, MUL), kd_tok, t3, free.get("kh"), fr)
        free["kd"] = [kh_tok]
        ar = q["ar"]
        ar_tok = [DVE(do(nc.vector.scalar_tensor_tensor, ar[:, :, 0:64], kkv, -1.0, fc(Pex), MUL, MUL), t2, kk_tok, old)]
        free["Pex"] = ar_tok[0:1]
        if lat:
            ar_tok.append(PO(do(nc.gpsimd.tensor_tensor, ar[:, :, 64:128], rT[:, :, tx], fc(Pin), MUL), t1,
                             [ztok["r", c] for c in range(8)], old))
        bh_tok = DVE(do(nc.vector.tensor_tensor, bh, tb_, Pinv, MUL), u, t3, free.get("bh"), fr)
        free["tb"] = free["Pinv"] = [bh_tok]
        pc_tok = DVE(do(nc.vector.tensor_copy, pcs[i % 2], fc(Pin)[:, :, 63 if d == 0 else 0]), t1, old)
        free["Pin"] = [pc_tok] + ar_tok[1:]
        yield

        def turn(dst, src, *deps):
            b = G.get()
            t = heads(b.ap, lambda s, c: do(nc.tensor.matmul, b.ap[s, 64 * c:64 * c + 64], fc(src)[:, c, :], ident[:, s], start=True, stop=True),
                      b.deps, *deps, at=())
            t = AC(do(nc.scalar.activation, dst, b.ap, ACT.Copy), t, old)
            b.done(t)
            return t

        w = 128 if lat else 64

        def pairs(put, lhs, *deps):
            b = two(G)
            bv = b.ap.rearrange("p (c n) -> p c n", c=8)
            t = heads(b.ap, lambda s, c: do(nc.tensor.matmul, bv[s, c, 0:w], fc(lhs)[s, c, :], ar[s, c, 0:w], start=True, stop=True),
                      b.deps, ar_tok, *deps)
            t = put(bv, t)
            b.done(t)
            return t

        def put_bt(bv, t):
            for h, x in enumerate(q["BT"]):
                s = slice(64 * h, 64 * h + 64)
                t1 = DVE(do(nc.vector.tensor_tensor, fc(x)[s, :, :], bv[s, :, 0:64], pair[s, 0:64].unsqueeze(1).to_broadcast([64, 8, 64]), MUL), t, old)
            if lat:
                t1 = DVE(do(nc.vector.tensor_tensor, fc(q["BTr"]), bv[:, :, 64:128], bc(pair[:, 64:128], 8, 64), MUL), t, old)
            return t1

        def put_ak(bv, t):
            return DVE(do(nc.vector.tensor_tensor, q["AKA"][:, :, 0:w], bv[:, :, 0:w], bc(pair[:, 0:w], 8, w), MUL), t, old)

        kt_tok = turn(q["ktok"], kh, kh_tok)
        yield
        bta_tok = pairs(put_bt, bh, bh_tok)
        yield
        b = G.get()
        t = heads(b.ap, lambda s, c: do(nc.tensor.matmul, b.ap[s, 64 * c:64 * c + 64], ar[s, c, 0:64], fc(bh)[s, c, :], start=True, stop=True),
                  b.deps, ar_tok, bh_tok)
        t = DVE(do(nc.vector.tensor_tensor, fc(q["X"]), fc(b.ap), bc(rwc[:, o:o + 64], 8, 64), MUL), t, old)
        b.done(t)
        x_t = DVE(do(nc.vector.tensor_tensor, fc(q["X"]), fc(q["X"]), bc(i64, 8, 64), ADD), t)
        xt_t = []
        for h, (x, y) in enumerate(zip(q["BT"], q["Xt"])):
            t = DVE(do(nc.vector.tensor_tensor, fc(y), fc(x), bc(rwc[:, o + 384:o + 448], 8, 64), MUL), bta_tok, old)
            xt_t.append(PO(do(nc.gpsimd.tensor_tensor, fc(y), fc(y), bc(ident[:, 64 * h:64 * h + 64], 8, 64), ADD), t))
        yield
        bt_tok = turn(q["btok"], bh, bh_tok)
        free["bh"] = [bt_tok]
        yield
        aka_tok = pairs(put_ak, kh, kh_tok)
        free["kh"] = [aka_tok]
        state[i] = dict(bta=bta_tok, aka=aka_tok, x=x_t, xt=xt_t, vt=vt_tok, kt=kt_tok, bt=bt_tok, ar=ar_tok, pc=pc_tok)
        yield

    sl = [slice(64 * c, 64 * c + 64) for c in range(8)]

    def own(pair, s):
        return fc(pair[s.start // 64])

    def invert(i):
        d, n = its[i]
        q, k = sets[i % 2], state[i]
        Xb, Xt, BT = (q[m] for m in ("X", "Xt", "BT"))
        x_t, xt_t = k["x"], k["xt"]
        for lv in range(1, 6):
            mask = rwc[:, 704 * d + 64 * lv:704 * d + 64 * lv + 64]
            b = X.get()
            t = heads(b.ap, lambda s, c: do(nc.tensor.matmul, b.ap[s, sl[c]], own(BT, s)[:, c, :], fc(Xb)[:, c, :], start=True, stop=True),
                      b.deps, k["bta"], x_t, at=(0,) if n < 4 and lv in (2, 3) else ())
            t1_t = DVE(do(nc.vector.tensor_tensor, fc(T1), fc(b.ap), bc(mask, 8, 64), MUL), t, xt_t, t1_read, fr)
            b.done(t1_t)
            yield
            if lv < 5:
                bx = X.get()
                t = heads(bx.ap, lambda s, c: do(nc.tensor.matmul, bx.ap[s, sl[c]], own(Xt, s)[:, c, :], fc(T1)[:, c, :], start=True, stop=True),
                          bx.deps, t1_t, xt_t, at=())
                x_t = DVE(do(nc.vector.tensor_tensor, Xb, Xb, bx.ap, ADD), t)
                bx.done(x_t)
            by = X.get()
            t = heads(by.ap, lambda s, c: do(nc.tensor.matmul, by.ap[s, sl[c]], fc(T1)[:, c, :], own(Xt, s)[:, c, :], start=True, stop=True),
                      by.deps, t1_t, xt_t, at=())
            for h in range(2):
                s = slice(64 * h, 64 * h + 64)
                xt_t = DVE(do(nc.vector.tensor_tensor, Xt[h][s, :], Xt[h][s, :], by.ap[s, :], ADD), t)
            by.done(xt_t)
            t1_read[:] = [xt_t]
            k["inv"], k["xd"] = xt_t, x_t
            yield

    def advance(i):
        d, n = its[i]
        q, k = sets[i % 2], state[i]
        Xt, BTr, AKA, ar, vtok = (q[m] for m in ("Xt", "BTr", "AKA", "ar", "vtok"))
        xt_t = k["inv"]
        first, last, Z = n == 0, n == 7, Zs[d]
        lat = n >= 4
        ck = n if d == 0 else (3 - n if n < 4 else 11 - n)
        b = X.get()
        for c in range(8):
            if c % 4 == 0:
                dense(b.ap, b.deps, at=64 * c)
            for hh in range(2):
                s = slice(64 * hh, 64 * hh + 64)
                if not first:
                    PE(do(nc.tensor.matmul, b.ap[s, sl[c]], ar[s, c, 0:64], fc(Z)[s, c, :], start=True, stop=False,
                          skip_group_check=True), b.deps, k["ar"], z_tok[d], inc=False)
                t = PE(do(nc.tensor.matmul, b.ap[s, sl[c]], AKA[s, c, 0:64], fc(vtok)[s, c, :], start=first, stop=True,
                          skip_group_check=True), b.deps, k["aka"], k["vt"], inc=(c == 7 and hh == 1))
        r_tok = AC(do(nc.scalar.activation, R, b.ap, ACT.Copy), t, r_read, fr)
        b.done(r_tok)
        yield
        b = X.get()
        t = heads(b.ap, lambda s, c: do(nc.tensor.matmul, b.ap[s, sl[c]], own(Xt, s)[:, c, :], fc(R)[:, c, :], start=True, stop=True),
                  b.deps, xt_t, r_tok, at=())
        r_read[:] = [t]
        u_tok = AC(do(nc.scalar.activation, U, b.ap, ACT.Copy), t, u_read, fr)
        b.done(u_tok)
        yield
        if not last:
            b = X.get()
            for c in range(8):
                if c % 4 == 0:
                    dense(b.ap, b.deps, at=64 * c)
                for hh in range(2):
                    s = slice(64 * hh, 64 * hh + 64)
                    PE(do(nc.tensor.matmul, b.ap[s, sl[c]], fc(q["btok"])[s, c, :], fc(U)[s, c, :], start=True, stop=False,
                          skip_group_check=True), b.deps, k["bt"], u_tok, inc=False)
                    t = PE(do(nc.tensor.matmul, b.ap[s, sl[c]], fc(q["ktok"])[s, c, :], fc(vtok)[s, c, :], start=False,
                              stop=True, skip_group_check=True), k["kt"], k["vt"], inc=(c == 7 and hh == 1))
            zb, zt = b, t
            yield
        if lat:
            tx = slice(64 * (ck - 4), 64 * (ck - 4) + 64)
            b = X.get()
            for c in range(8):
                if c % 4 == 0:
                    dense(b.ap, b.deps, at=64 * c)
                for hh in range(2):
                    s = slice(64 * hh, 64 * hh + 64)
                    PE(do(nc.tensor.matmul, b.ap[s, sl[c]], fc(Z)[s, c, :], ar[s, c, 64:128], start=True, stop=False,
                          skip_group_check=True), b.deps, z_tok[d], k["ar"], inc=False)
                    PE(do(nc.tensor.matmul, b.ap[s, sl[c]], fc(U)[s, c, :], fc(BTr)[s, c, :], start=False, stop=False,
                          skip_group_check=True), u_tok, inc=False)
                    t = PE(do(nc.tensor.matmul, b.ap[s, sl[c]], fc(vtok)[s, c, :], AKA[s, c, 64:128], start=False,
                              stop=True, skip_group_check=True), k["aka"], k["vt"], inc=(c == 7 and hh == 1))
            if ck not in y_tok:
                y_tok[ck] = AC(do(nc.scalar.activation, yT[:, :, tx], fc(b.ap), ACT.Copy), t, fr)
            else:
                y_tok[ck] = DVE(do(nc.vector.tensor_tensor, yT[:, :, tx], yT[:, :, tx], fc(b.ap), ADD), t, y_tok[ck])
            b.done(y_tok[ck])
        u_read[:] = [t]
        if not last:
            pc = bcol(pcs[i % 2], 8, 64)
            if first:
                z_tok[d] = DVE(do(nc.vector.tensor_tensor, fc(Z), fc(zb.ap), pc, MUL), zt, k["pc"], fr)
                zb.done(z_tok[d])
            else:
                z1 = DVE(do(nc.vector.tensor_tensor, Z, Z, zb.ap, ADD), zt, t)
                zb.done(z1)
                z_tok[d] = DVE(do(nc.vector.tensor_tensor, fc(Z), fc(Z), pc, MUL), z1, k["pc"])
        done[i % 2] = [t, z_tok[d], xt_t, k["xd"]]
        yield

    def burst(n):
        rest(limited(filler, n))
        ada_end()

    preps = [prepare(i) for i in range(16)] + [iter(())] * 3

    def late(i):
        early = limited(preps[i + 1], 3)
        rest(limited(preps[i], 2))
        for plan in ("e", "le", "l", "le", "l", "l", "l"):
            for p in plan:
                next(early if p == "e" else preps[i], None)
            yield

    burst(8)
    rest(limited(preps[0], 3))
    rest(late(0))
    burst(7)
    run_all((invert(0), 1), (late(1), 1))
    for i in range(16):
        burst(6)
        run_all((chain(advance(i), late(i + 2)), 1), (invert(i + 1) if i < 15 else iter(()), 1))
    rest(filler)
    ada_end()

    f1 = fence()
    tmps.free += [(0, [f1]), (1, [f1])]
    gl = counter()
    gup, gup2 = A("gup"), A("gup2")
    AC.dma(gup, io["g_up"][0:128, :], gl, f1)
    gl_tok = AC.dma(gup2[96:128, :], io["g_up"][128:160, :], gl, f1)
    lng, lnb = cst("lnx_g", 8), cst("lnx_b", 8)
    open_gate(f1)
    HA.tok = [[] for _ in range(16)]
    mix_tok = AC.dma(mix[:, 0:8, :], io["mix_keep"], counter(), f1, mix_saved)
    mu = A("mu")
    wide = Pool([A("ob")[:, i, :] for i in range(2)])
    slim = Pool([A("ork")[:, i, :] for i in range(4)])
    var_tok = []

    def out_mean(p):
        y = yT[:, 2 * p:2 * p + 2, :].rearrange("p c n -> p (c n)")
        b = X.get()
        m = PE(do(nc.tensor.matmul, b.ap, blk, y, start=True, stop=True), f1, b.deps)
        t = DVE(do(nc.vector.scalar_tensor_tensor, y, b.ap, -1.0 / 64, y, MUL, ADD), m)
        yield
        sq = wide.get()
        t = AC(do(nc.scalar.activation, sq.ap, y, ACT.Square), t, sq.deps, f1)
        m = PE(do(nc.tensor.matmul, b.ap, blk, sq.ap, start=True, stop=True), t)
        sq.done(m)
        var_tok.append(DVE(do(nc.vector.tensor_scalar, mu[:, 512 * p:512 * p + 512], b.ap, 1.0 / 64, 64e-5, MUL, ADD), m, f1))
        b.done(var_tok[-1])

    def out_rest(c, rs_tok):
        pool, y = (G, X)[c % 2], yT[:, c, :]
        b = pool.get()
        for d in range(2):
            m = PE(do(nc.tensor.matmul, b.ap[:, 256 * d:256 * d + 256], aup[:, 128 * c:128 * c + 128], lora[d][:, 1, 256:512],
                      start=True, stop=True, skip_group_check=True), f1, b.deps, inc=(d == 1))
        th = wide.get()
        t = [AC(do(nc.scalar.activation, th.ap[:, 256 * d:256 * d + 256], b.ap[:, 256 * d:256 * d + 256], ACT.Tanh,
                   bias=a0h[:, 8 * d + c:8 * d + c + 1], scale=0.5), m, th.deps, f1) for d in range(2)]
        b.done(t)
        yield
        rk = slim.get()
        t = DVE(do(nc.vector.tensor_tensor, rk.ap, th.ap[:, 0:256], th.ap[:, 256:512], ADD), t, rk.deps, f1)
        th.done(t)
        t = DVE(do(nc.vector.tensor_scalar, rk.ap, rk.ap, hk[:, c:c + 1], hc[:, c:c + 1], MUL, ADD), t)
        t = DVE(do(nc.vector.tensor_tensor, rk.ap, rk.ap, kT[:, c, 256:512], MUL), t)
        t = DVE(do(nc.vector.scalar_tensor_tensor, rk.ap, rk.ap, rkc[:, c:c + 1], rT[:, c, :], MUL, MUL), t)
        yield
        b = pool.get()
        g = b.ap[:, 256:512]
        PE(do(nc.tensor.matmul, g, gup[:, 128 * c:128 * c + 128], gd[:, 0, :], start=True, stop=False, skip_group_check=True),
           gl_tok, ztok["gd", 0], b.deps, inc=False)
        PE(do(nc.tensor.matmul, g, gup2[96:128, 128 * c:128 * c + 128], gd[96:128, 1, :], start=False, stop=True,
              skip_group_check=True), ztok["gd", 1], inc=False)
        m = PE(do(nc.tensor.matmul, b.ap[:, 0:256], blk, rk.ap, start=True, stop=True, skip_group_check=True), t)
        t = DVE(do(nc.vector.tensor_tensor, rk.ap, b.ap[:, 0:256], vT[:, c, 256:512], MUL), m)
        yield
        t = DVE(do(nc.vector.scalar_tensor_tensor, y, y, lng[:, c:c + 1], mu[:, 256 * c:256 * c + 256], MUL, MUL), rs_tok)
        t = DVE(do(nc.vector.scalar_tensor_tensor, y, y, lnb[:, c:c + 1], rk.ap, ADD, ADD), t)
        rk.done(t)
        t = DVE(do(nc.vector.tensor_tensor, y, y, g, MUL), t)
        b.done(t)
        split(HA, 8 + c, 1, mix[:, 8 + c:9 + c, :], t, f1)

    run_all(*[(out_mean(p), 1) for p in range(4)])
    t = AC(do(nc.scalar.activation, mu, mu, ACT.Sqrt), var_tok)
    rs_tok = DVE(do(nc.vector.reciprocal, mu, mu), t)
    for c in range(0, 8, 4):
        split(HA, c, 4, mix[:, c:c + 4, :], f1, mix_tok)
    split_ahead()
    rolling([out_rest(c, rs_tok) for c in range(8)], 4)

    f2 = fence()
    xl = counter()
    x_tok = AC.dma(xt, io["xT"], xl, f2)

    xdeps = {}

    sums = {}

    def add_squares():
        sq, t = sums.pop("wait")
        for c in range(2):
            sums["tok"] = PE(do(nc.tensor.matmul, sums["bank"].ap[:, 0:T], ones, sq.ap[:, c, :], start=sums["first"], stop=False,
                                skip_group_check=True), t, sums["bank"].deps, inc=(c == 1))
            sums["first"] = False
        sq.done(sums["tok"])

    def root_of_sums():
        add_squares()
        return inverse_root(sums["bank"], sums["tok"], 16)

    def add_to_x(gate, gtok, squares=False):
        if squares:
            sums.update(bank=X.get(), first=True)

        def make(n):
            def ev(banks, tok):
                for fb in range(2):
                    c = 2 * n + fb
                    if gate is None:
                        t = DVE(do(nc.vector.tensor_tensor, xt[:, c, :], xt[:, c, :],
                                                                     banks[0].ap[:, 256 * fb:256 * fb + 256], ADD),
                                tok, x_tok, xdeps.get(c))
                    else:
                        t = DVE(do(nc.vector.scalar_tensor_tensor, xt[:, c, :], banks[0].ap[:, 256 * fb:256 * fb + 256], gate[:, c:c + 1], xt[:, c, :], MUL, ADD),
                            tok, x_tok, gtok, xdeps.get(c))
                    xdeps[c] = t
                banks[0].done(t)
                if squares:
                    if "wait" in sums:
                        add_squares()
                    sq = work4.get()
                    sums["wait"] = (sq, AC(do(nc.scalar.activation, sq.ap[:, 0:2, :], xt[:, 2 * n:2 * n + 2, :], ACT.Square),
                                           xdeps[2 * n], xdeps[2 * n + 1], sq.deps))
            return ev
        return make

    work4.free = [(i, [f2]) for i, _ in work4.free]
    ev = add_to_x(mods[:, 2, 0, :], mod_tok[23], True)
    for n in range(8):
        rest(gemm("w_out", n, range(4), xonly, 1, ev(n)))
    g2s = plus_one(gs[:, 0:16], cst("norm2", 16), mods[:, 4, 0, :], mod_tok[39], fence())
    r = root_of_sums()
    normed(xt, r, gs[:, 0:16], mods[:, 3, 0, :], HA, [g2s, mod_tok[31], fence()])

    bon = [(0, 256 * fb, "B", 128 * fb, HB, 0) for fb in range(2)]

    def swiglu(gate_up, pos):
        (a, ta), (b, tb) = gate_up
        s = work4.get()
        th, v = (s.ap[:, 2 * i:2 * i + 2, :] for i in range(2))
        av, bv = (q.ap.rearrange("p (c n) -> p c n", c=2) for q in (a, b))
        t = tanh_half(th, av, ta, s.deps)
        t = DVE(do(nc.vector.scalar_tensor_tensor, v, th, 1.0, av, ADD, MUL), t)
        a.done(t)
        t = DVE(do(nc.vector.scalar_tensor_tensor, v, v, 0.5, bv, MUL, MUL), t, tb)
        b.done(t)
        s.done(split(HB, pos, 2, v, t, hb_dep))

    held = {}

    def keep(name):
        def ev(banks, tok):
            held[name] = (banks[0], tok)
        return ev

    for part, (k0, k1) in enumerate(((0, 4), (4, 8), (8, 11))):
        hb_dep = [PE.last()]
        for j in range(2 * k0, 2 * k1):
            rest(gemm("ffn1", j, range(4), xonly, 1, keep("a")))
            rest(gemm("ffn3", j, range(4), xonly, 1, keep("b")))
            swiglu((held["a"], held["b"]), 2 * (j - 2 * k0))
        ev_x = add_to_x(mods[:, 5, 0, :], mod_tok[47], part == 2)
        for n in range(8):
            rest(gemm("ffn2", n, range(k0, k1), bon, 1, ev_x(n), kbase=k0))

    def norm_in_place(gain, xdone):
        r = root_of_sums()
        toks = []
        for c in range(16):
            toks.append(DVE(do(nc.vector.scalar_tensor_tensor, xt[:, c, :], xt[:, c, :], gain[:, c:c + 1], r.ap, MUL, MUL),
                            r.tok, xdone))
        r.done(toks)
        for c in range(16):
            xdeps[c] = toks[c]
        return toks

    norm_in_place(cst("final1", 16), [list(xdeps.values()), fence()])

    work2 = None

    def silu_from(dst, bank, tok, *deps):
        b = bank.ap.rearrange("p (c n) -> p c n", c=2)
        t = tanh_half(dst, b, tok, *deps)
        t = DVE(do(nc.vector.scalar_tensor_tensor, dst, dst, 1.0, b, ADD, MUL), t)
        bank.done(t)
        return DVE(do(nc.vector.tensor_scalar, dst, dst, 0.5, None, MUL), t)

    def tile(pool, name, nt, kind, acts, finish):
        box = {}

        def ev(banks, tok):
            b = pool.get()
            box["b"] = b
            b.tok = finish(b.ap, banks[0], tok, b.deps)
        outs = [(0, 256 * i, kind, 128 * i if kind == "B" else 0, acts, i) for i in range(2)]
        return box, gemm(name, nt, range(4), outs, 1, ev)

    def plain(scale=1.0):
        def f(dst, bank, tok, deps):
            t = AC(do(nc.scalar.activation, dst, bank.ap.rearrange("p (c n) -> p c n", c=2), ACT.Copy, scale=scale), tok, deps)
            bank.done(t)
            return t
        return f

    def gated(dst, bank, tok, deps):
        return silu_from(dst, bank, tok, deps)

    def softmax_rows(p, width, scale, k, *deps):
        mx, nm, rs = (cols[:, k + i:k + i + 1] for i in range(3))
        t = DVE(do(nc.vector.tensor_reduce, mx, p, AX.X, MAX), *deps)
        t = DVE(do(nc.vector.tensor_scalar, nm, mx, -scale, None, MUL), t)
        t = AC(do(nc.scalar.activation, p, p, ACT.Exp, bias=nm, scale=scale, accum_out=rs), t)
        t = DVE(do(nc.vector.reciprocal, rs, rs), t)
        return DVE(do(nc.vector.tensor_scalar, p, p, rs, None, MUL), t)

    def mem_head(q, k, v, g, ch, pool, big):
        b = X.get()
        for qb in range(2):
            for dc in range(2):
                t = PE(do(nc.tensor.matmul, b.ap[:, 256 * qb:256 * qb + 256], q.ap[:, dc, 128 * qb:128 * qb + 128],
                                                        k.ap[:, dc, :], start=(dc == 0), stop=(dc == 1)),
                       q.tok, k.tok, b.deps, inc=(qb == 1 and dc == 1))
        p = big.get()
        t1 = AC(do(nc.scalar.activation, p.ap[:, 0:512], b.ap, ACT.Copy), t, p.deps)
        b.done(t1)
        yield
        tt = [softmax_rows(p.ap[:, 256 * qb:256 * qb + 256], 256, 1.0 / 16, 8 * qb + 4 * (ch % 4), t1) for qb in range(2)]
        b = X.get()
        for qb in range(2):
            for mb in range(2):
                t = PE(do(nc.tensor.transpose, b.ap[:, 256 * mb + 128 * qb:256 * mb + 128 * qb + 128],
                                                           p.ap[:, 256 * qb + 128 * mb:256 * qb + 128 * mb + 128], ident),
                       tt, b.deps, inc=(qb == 1 and mb == 1))
        t1 = AC(do(nc.scalar.activation, p.ap[:, 0:512], b.ap, ACT.Copy), t)
        b.done(t1)
        yield
        b = X.get()
        for dc in range(2):
            for mb in range(2):
                t = PE(do(nc.tensor.matmul, b.ap[:, 256 * dc:256 * dc + 256], v.ap[:, mb, 128 * dc:128 * dc + 128],
                                                        p.ap[:, 256 * mb:256 * mb + 256], start=(mb == 0), stop=(mb == 1)),
                       t1, v.tok, b.deps, inc=(dc == 1 and mb == 1))
        p.done(t)
        t2 = DVE(do(nc.vector.tensor_tensor, mix[:, ch:ch + 2, :], b.ap.rearrange("p (c n) -> p c n", c=2), g.ap, MUL), t, g.tok, mix_dep)
        b.done(t2)
        q.done(t)
        k.done(t)
        v.done(t)
        g.done(t2)
        yield

    def pipeline(groups, ratio=1, before=None):
        for tiles, after in groups:
            def products():
                for _, g in tiles:
                    yield from g
            if before is None:
                rest(products())
            else:
                run_all((products(), ratio), (before, 1))
            before = after([b["b"] for b, _ in tiles])
        return before

    l_mem = [counter() for _ in range(4)]

    def recall(pool, lay, n, i):
        box = {}

        def load():
            b = pool.get()
            box["b"] = b
            b.tok = AC.dma(b.ap, io["mem_keep"][lay, n].rearrange("p (c n) -> p c n", c=2), l_mem[i], b.deps, mem_saved[lay, n])
            yield
        return box, load()

    def mem_groups(lay, wname, q0, g0, pool, big):
        res = []
        for h in range(4):
            tiles = [recall(pool, lay, h, h % 2), recall(pool, lay, 4 + h, 2 + h % 2),
                     tile(pool, wname, q0 + h, "B", HA, plain()), tile(pool, wname, g0 + h, "B", HA, gated)]
            res.append((tiles, lambda bs, h=h: mem_head(bs[2], bs[0], bs[1], bs[3], 16 + 2 * h, pool, big)))
        return res

    def pool2(name, n):
        v = A(name)
        return Pool([v[:, 512 * i:512 * i + 512].rearrange("p (c n) -> p c n", c=2) for i in range(n)])

    f3 = fence()
    r = rms(xt, 16, None, work4, by=xdeps)
    normed(xt, r, cst("norm_a", 16), None, HA, f3)
    f4 = fence()
    mix_dep = f4
    pl = counter()
    pl_tok = AC.dma(phc[:, 0:512], io["ret_c"], pl, f4)
    cos2, sin2 = phc[:, 0:256], phc[:, 256:512]
    dec = Pool([phc[:, 512 + 512 * i:1024 + 512 * i] for i in range(2)])
    for i in range(2):
        dec.free[i] = (i, [f4])
    dsem = [counter(), counter()]
    w2 = pool2("work", 11)
    big = Pool([A("work")[:, 5632 + 1024 * i:5632 + 1024 * i + 1024] for i in range(2)])
    for pool in (w2, big):
        pool.free = [(i, [f4]) for i, _ in pool.free]

    def rotated(scale):
        def f(dst, bank, tok, deps):
            out_, done = [], []
            dead.append(deps)
            for c in range(2):
                t1, t2 = rope(dst[:, c, :], bank, 256 * c, 256, scale, tok, cst("rot128", 128), cos2, sin2, pl_tok)
                done.append(t1)
                out_.append(t2)
            bank.done(done)
            return out_
        return f

    def ret_head(q, k, v, g, c, h, last):
        db = dec.get()
        d_tok = AC.dma(db.ap, io["decay"][h], dsem[db.i], db.deps)
        b = X.get()
        for kb in range(2):
            t = PE(do(nc.tensor.matmul, b.ap[:, 256 * kb:256 * kb + 256], k.ap[:, c, 128 * kb:128 * kb + 128], q.ap[:, c, :],
                                             start=True, stop=True), q.tok, k.tok, b.deps, inc=(kb == 1))
        s = big.get()
        t1 = DVE(do(nc.vector.tensor_tensor, s.ap[:, 0:512], b.ap, db.ap, MUL), t, d_tok, s.deps)
        b.done(t1)
        db.done(t1)
        yield
        b = X.get()
        for ec in range(2):
            for kb in range(2):
                t2 = PE(do(nc.tensor.matmul, b.ap[:, 256 * ec:256 * ec + 256], v.ap[:, kb, 128 * ec:128 * ec + 128],
                                                         s.ap[:, 256 * kb:256 * kb + 256], start=(kb == 0), stop=(kb == 1)),
                        t1, v.tok, b.deps, inc=(ec == 1 and kb == 1))
        o = mix[:, 2 * h:2 * h + 2, :]
        bv = b.ap.rearrange("p (c n) -> p c n", c=2)
        ta = AC(do(nc.scalar.activation, s.ap[:, 512:1024], b.ap, ACT.Square), t2)
        yield
        b2 = X.get()
        for ec in range(2):
            t = PE(do(nc.tensor.matmul, b2.ap[:, 0:256], ones, s.ap[:, 512 + 256 * ec:768 + 256 * ec], start=(ec == 0), stop=(ec == 1)),
                   ta, b2.deps, inc=(ec == 1))
        rr = s.ap[:, 0:256]
        t = DVE(do(nc.vector.tensor_scalar, rr, b2.ap[:, 0:256], 1.0 / 256, 1e-6, MUL, ADD), t, t2)
        b2.done(t)
        t = AC(do(nc.scalar.activation, rr, rr, ACT.Sqrt), t)
        t = DVE(do(nc.vector.reciprocal, rr, rr), t)
        t = DVE(do(nc.vector.tensor_tensor, o, bv, rr.unsqueeze(1).to_broadcast([128, 2, 256]), MUL), t, mix_dep)
        b.done(t)
        s.done(t)
        t = PO(do(nc.gpsimd.tensor_tensor, o, o, g.ap, MUL), t, g.tok)
        v.done(t2)
        g.done(t)
        if last:
            q.done(t2)
            k.done(t2)
        yield

    groups = mem_groups(0, "w_in_a", 24, 28, w2, big)
    for p in range(4):
        tiles = [tile(w2, "w_in_a", p, "B", HA, rotated(1.0)), tile(w2, "w_in_a", 4 + p, "B", HA, rotated(128 ** -0.5)),
                 tile(w2, "w_in_a", 8 + 2 * p, "A", HA, plain()), tile(w2, "w_in_a", 16 + 2 * p, "B", HA, gated),
                 tile(w2, "w_in_a", 9 + 2 * p, "A", HA, plain()), tile(w2, "w_in_a", 17 + 2 * p, "B", HA, gated)]

        def heads2(bs, p=p):
            q, k, v0, g0, v1, g1 = bs
            yield from ret_head(q, k, v0, g0, 0, 2 * p, False)
            yield from ret_head(q, k, v1, g1, 1, 2 * p + 1, True)
        groups.append((tiles, heads2))
    rest(pipeline(groups, 2))

    def project(name):
        f = fence()
        for k in range(6):
            c = 4 * k
            split(HA if k < 4 else HB, c % 16, 4, mix[:, c:c + 4, :], f, eng=(DVE, PO)[k % 2])
        work4.free = [(i, [f]) for i, _ in work4.free]
        wide = Wide(HA, HB)
        ev = add_to_x(None, None, True)
        for n in range(8):
            rest(gemm(name, n, range(6), [(0, 256 * fb, "B", 128 * fb, wide, 0) for fb in range(2)], 1, ev(n)))

    class Wide:
        def __init__(self, a, b):
            self.hi, self.lo = Pick(a.hi, b.hi), Pick(a.lo, b.lo)
            self.tok = a.tok + b.tok

    class Pick:
        def __init__(self, a, b):
            self.a, self.b = a, b

        def __getitem__(self, key):
            p, c, n = key
            return self.a[p, c, n] if c < 16 else self.b[p, c - 16, n]

    project("w_out_a")

    f5 = fence()
    r = root_of_sums()
    rest(normed_steps(xt, r, cst("norm_b", 16), None, HA, f5, False))
    f6 = fence()
    mix_dep = f6
    for pool in (w2, big):
        pool.free = [(i, [f6]) for i, _ in pool.free]
    rest(pipeline(mem_groups(1, "w_in_b", 32, 36, w2, big), before=normed_steps(xt, r, cst("kv_g", 16), None, HB, f6), ratio=3))
    f8 = fence()
    xs = counter()
    xs_tok = AC.dma(io["x_keep"], xt, xs, f8)
    pl = counter()
    pm_tok = AC.dma(phc[:, 0:1152], io["dil_c"], pl, f8)
    w3 = Pool([A("work")[:, 512 * i:512 * i + 512].rearrange("p (c n) -> p c n", c=2) for i in range(15)]
              + [A("xw")[:, 512 * i:512 * i + 512].rearrange("p (c n) -> p c n", c=2) for i in range(2)])
    w3.free = [(i, [f8, xs_tok]) for i, _ in w3.free]
    xw = A("xw")
    pb = Pool([xw[:, 1024:1792], xw[:, 1792:2560]])
    pt9 = Pool([xw[:, 2560:3328], xw[:, 3328:4096]])
    for pool in (pb, pt9):
        pool.free = [(i, [f8, xs_tok]) for i, _ in pool.free]

    def dil_head(qs, ks, vs, g, c, h, last):
        ob = X.get()
        for qb in range(2):
            nk = qb + 1
            w = 128 * nk
            b = two(X) if qb else X.get()
            for gi in range(3):
                t = PE(do(nc.tensor.matmul, b.ap[:, w * gi:w * gi + w], qs[gi].ap[:, c, 128 * qb:128 * qb + 128],
                                                 ks[gi].ap[:, c, 0:w], start=True, stop=True),
                       [q.tok for q in qs], [k.tok for k in ks], b.deps, inc=(gi == 2))
            p = pb.get()
            pv = p.ap[:, 0:3 * w]
            mk = phc[:, 384 * qb:384 * qb + 3 * w]
            t1 = DVE(do(nc.vector.tensor_tensor, pv, b.ap[:, 0:3 * w], mk, ADD), t, p.deps, pm_tok)
            b.done(t1)
            yield
            t2 = softmax_rows(pv, 3 * w, 128 ** -0.5, 4 * ((2 * h + qb) % 8), t1)
            b = two(X) if qb else X.get()
            n = 3 * nk
            for i in range(n):
                t = PE(do(nc.tensor.transpose, b.ap[:, 128 * i:128 * i + 128], pv[:, 128 * i:128 * i + 128], ident),
                       t2, b.deps, inc=(i == n - 1))
            p.done(t)
            pt = pt9.get()
            t1 = AC(do(nc.scalar.activation, pt.ap[:, 0:128 * n], b.ap[:, 0:128 * n], ACT.Copy), t, pt.deps)
            b.done(t1)
            yield
            for i in range(n):
                gi, kb = divmod(i, nk)
                t = PE(do(nc.tensor.matmul, ob.ap[:, 128 * qb:128 * qb + 128], vs[gi].ap[:, kb, 128 * c:128 * c + 128], pt.ap[:, 128 * i:128 * i + 128],
                    start=(i == 0), stop=(i == n - 1)), t1, [v.tok for v in vs], ob.deps, inc=(i == n - 1))
            pt.done(t)
        t2 = DVE(do(nc.vector.tensor_tensor, mix[:, h, :], ob.ap[:, 0:256], g.ap[:, c, :], MUL), t, g.tok, mix_dep)
        ob.done(t2)
        if last:
            for x in qs + ks + vs:
                x.done(t)
            g.done(t2)
        yield

    groups = []
    for p in range(8):
        tiles = [tile(w3, "w_in_b", 8 * gi + p, "B", HA, plain()) for gi in range(3)]
        tiles += [tile(w3, "w_kv", 16 * gi + p, "B", HB, plain()) for gi in range(3)]
        tiles += [tile(w3, "w_kv", 16 * gi + 8 + p, "A", HB, plain()) for gi in range(3)]
        tiles += [tile(w3, "w_in_b", 24 + p, "B", HA, gated)]

        def heads3(bs, p=p):
            for c in range(2):
                yield from dil_head(bs[0:3], bs[3:6], bs[6:9], bs[9], c, 2 * p + c, c == 1)
        groups.append((tiles, heads3))
    rest(pipeline_tight(groups, run_all, rest))
    f9 = fence()
    xr = counter()
    x_tok = AC.dma(xt, io["x_keep"], xr, f9, xs_tok)
    project("w_out_b")
    toks = norm_in_place(cst("final2", 16), [list(xdeps.values()), fence()])
    ol = counter()
    for c in range(0, 16, 4):
        o_tok = SP.dma(out[:, c:c + 4, :], xt[:, c:c + 4, :], ol, toks[c + 3])
    SP.queue.append((SP.waits([o_tok, xs_tok]), None, None, 0))
    return engines, rec


def pipeline_tight(groups, run_all, rest):
    before = None
    for tiles, after in groups:
        def part(ts):
            for _, g in ts:
                yield from g
        if before is None:
            rest(part(tiles))
        else:
            run_all((part(tiles[:7]), 2), (before, 1))
            rest(part(tiles[7:]))
        before = after([b["b"] for b, _ in tiles])
    return before


COLS = {}
NCONST = 0
for _n, _w in (("ident", 128), ("ones", 128), ("blk", 128), ("rot32", 128), ("rot128", 128), ("c", 32), ("ada_b", 96),
               ("norm1", 16), ("norm2", 16), ("final1", 16), ("norm_a", 16), ("norm_b", 16), ("mem_g", 16), ("kv_g", 16),
               ("final2", 16), ("ts", 56), ("a0", 16), ("k_k", 8), ("k_a", 8), ("r_k", 8), ("lnx_g", 8), ("lnx_b", 8),
               ("sink", 16), ("sel", 2)):
    COLS[_n] = NCONST
    NCONST += _w


def memory(nc, base):
    m = {}

    def at(name, off, shape, dt=F32):
        m[name] = nc.alloc_sbuf_tensor_at(name, [128, *shape], dt, offset=base + off)[:]

    K = 1024
    at("raw", 0, [NRAW, 1024])
    at("wh", 24 * K, [NW, 1024], F32R)
    at("wl", 40 * K, [NW, 1024], F32R)
    x, hah, hal, hbh, hbl, mx = 56 * K, 72 * K, 88 * K, 104 * K, 120 * K, 136 * K
    at("x", x, [16, T])
    at("xk", x, [8, 512])
    at("xw", x, [4096])
    at("hah", hah, [16, T], F32R)
    at("hal", hal, [16, T], F32R)
    at("hbh", hbh, [16, T], F32R)
    at("hbl", hbl, [16, T], F32R)
    at("mix", mx, [24, T])
    c = 160 * K
    at("const", c, [NCONST])
    at("mod", c + 4128, [192])
    at("sc", c + 4896, [32])
    at("gs", c + 5024, [32])
    at("tsr", c + 5152, [28])
    at("cols", c + 5280, [64])
    c += 5664
    at("phc", c, [1536])
    at("rwc", c, [1472])
    c += 6144
    at("rst", c, [2, T])
    at("tm", c + 2048, [4, T])
    c += 6144
    at("work", c, [7680])
    wk = c
    at("kk", hah, [8, 512])
    at("hal32", hal, [4096])
    at("hbl32", hbl, [4096])
    for i, (n, w) in enumerate((("lw", 1024), ("Pex", 512), ("Pin", 512), ("Pinv", 512), ("ab", 512), ("tb", 512), ("kd", 512))):
        at(n, hal + (0 if i == 0 else 4096 + 2048 * (i - 1)), [w])
    at("wup", hbl, [1024])
    at("aup", hbl + 4096, [1024])
    at("w0r", hbl + 8192, [1024])
    at("pad", c - 6144, [2, 512])
    at("bh", hbl + 12288, [512])
    at("kh", hbl + 14336, [512])
    at("hb_r", hbh, [8, T])
    at("hb_q", hbh + 8192, [8, T])
    for n, o, w in (("btok", hbh + 8192, [512]), ("ktok", hbh + 10240, [512]), ("vtok", hbh + 12288, [512]), ("X", hbh + 14336, [512]),
                    ("ar", wk + 16384, [8, 128]), ("BTr", wk + 20480, [512]), ("AKA", mx + 16 * K, [8, 128]),
                    ("Xtb", wk + 22528, [512]), ("Xta", mx + 20 * K, [512]), ("BTa", mx, [512]), ("BTb", mx + 2 * K, [512])):
        at(n + "0", o, w)
    for n, o, w in (("ar", 24, [8, 128]), ("BTr", 28, [512]), ("Xtb", 30, [512]), ("AKA", 32, [8, 128]), ("X", 36, [512]), ("Xta", 38, [512]),
                    ("btok", 40, [512]), ("ktok", 42, [512]), ("vtok", 44, [512])):
        at(n + "1", o * K, w)
    at("BTa1", mx + 4 * K, [512])
    at("BTb1", mx + 6 * K, [512])
    for n, o in (("T1", 46), ("R", 48), ("U", 50), ("Z0", 52), ("Z1", 54)):
        at(n, o * K, [512])
    at("sc16", mx + 22 * K, [512])
    at("gup", wk + 16384, [1024])
    at("gup2", wk + 20480, [1024])
    at("nk", 24 * K, [8, 512])
    at("mu", hbh + 8192, [2048])
    at("ob", hbl + 8192, [2, 512])
    at("ork", hbl + 12288, [4, T])
    assert wk + 7680 * 4 + base <= 229344, wk + 7680 * 4 + base
    return m


def bass_program(nc, io, out):
    with ExitStack() as ctx:
        sems = {n: ctx.enter_context(nc.semaphore(n)) for n in [f"e{i}" for i in range(5)] + [f"d{i}" for i in range(60)]}
        base = -(-nc.sbuf_base // 32) * 32
        mem = memory(nc, base)
        mem["ps"] = ctx.enter_context(nc.psum_tensor("ps", [128, 8, 512], F32))[:]
        _, order = build(nc, io, out, sems, mem, None)
        engines, _ = build(nc, io, out, sems, mem, order)
        block = ctx.enter_context(nc.Block())
        sp, pe, dve, act, pool = engines
        block.sync(lambda e: sp.emit(e))
        block.tensor(lambda e: pe.emit(e))
        block.vector(lambda e: dve.emit(e))
        block.scalar(lambda e: act.emit(e))
        block.gpsimd(lambda e: pool.emit(e))


def tables():
    f = np.float32
    p = np.arange(128)
    t = np.arange(T)
    c = {}
    c["ident"] = np.eye(128, dtype=f)
    c["sel"] = (p[:, None] % 32 == 16 * np.arange(2)[None, :]).astype(f)
    c["ones"] = np.ones((128, 128), f)
    c["blk"] = (p[:, None] // 64 == p[None, :] // 64).astype(f)

    def rot(half):
        r = np.zeros((128, 128), f)
        for i in range(128):
            if i % (2 * half) < half:
                r[i + half, i] = -1
            else:
                r[i - half, i] = 1
        return r

    c["rot32"], c["rot128"] = rot(16), rot(64)
    d = p % 64
    freqs = (f(1.0) / (f(10000.0) ** (np.arange(16, dtype=f) / f(16)))).astype(f)
    pos = np.where((d < 32)[:, None], (t // 64)[None, :], (t % 64)[None, :]).astype(f)
    ang = (pos * freqs[d % 16][:, None]).astype(f)
    q = np.arange(128)[:, None, None] + 128 * np.arange(2)[None, :, None]
    amask = np.where(np.abs(q - t[None, None, :]) <= 128, 0.0, NEG).astype(f)
    c["attn_c"] = np.concatenate([np.cos(ang), np.sin(ang), amask.reshape(128, 512)], 1).astype(f)
    inv = (f(1.0) / (f(10000.0) ** np.linspace(0.0, 1.0, 64, dtype=f))).astype(f)
    ang = (t.astype(f)[None, :] * inv[p % 64][:, None]).astype(f)
    c["ret_c"] = np.concatenate([np.cos(ang), np.sin(ang)], 1).astype(f)
    log_g = np.log1p(-(f(2.0) ** (f(-5.0) - np.arange(8, dtype=f)))).astype(f)
    k = p[:, None, None] + 128 * np.arange(2)[None, :, None]
    rel = (t[None, None, :] - k).astype(f)
    c["decay"] = np.stack([np.where(rel >= 0, np.exp(np.maximum(rel, 0) * g), 0).astype(f).reshape(128, 512) for g in log_g])
    parts = []
    for qb in range(2):
        for dil in (1, 4, 16):
            dist = (128 * qb + p)[:, None] - np.arange(128 * (qb + 1))[None, :]
            ok = (dist >= 0) & (dist % dil == 0) & (dist // dil <= 128)
            parts.append(np.where(ok, 0.0, NEG).astype(f))
    c["dil_c"] = np.concatenate(parts, 1)
    i, j = (p % 64)[:, None], np.arange(64)[None, :]
    parts = []
    for back in range(2):
        for n in (1, 2, 4, 8, 16, 32):
            a, b = (i, j) if not back else (j, i)
            parts.append((a // (2 * n) == b // (2 * n)) & (a // n % 2 == 1) & (b // n % 2 == 0))
        a, b = (j, i) if not back else (i, j)
        parts.append((a // 2 == b // 2) & (a % 2 == 1) & (b % 2 == 0))
        parts += [j > i, j >= i] if not back else [j < i, j <= i]
        parts += [i <= j, i < j] if not back else [i >= j, i > j]
    parts.append(i == j)
    c["rwkv_c"] = np.concatenate([x.astype(f) for x in parts], 1)
    return c


def columns(v):
    return np.asarray(v).reshape(-1, 128).T


def tiled(w, width=256):
    k, n = w.shape
    return np.ascontiguousarray(w.reshape(k // 512, 4, 128, n // width, width).transpose(3, 0, 2, 1, 4))


def kernel(**inputs):
    import concourse.bacc as _bacc
    from concourse.bass_utils import run_bass_kernel_spmd as _run

    g = {k: np.asarray(v) for k, v in inputs.items()}
    tab = tables()
    heads = [h for c in range(2) for i in range(4) for h in (8 * c + i, 8 * c + 4 + i)]
    w_in, w_out = g["w_in"][0], g["w_out"][0]
    wq = w_in[:, 0:1024].reshape(2048, 16, 64)[:, heads].reshape(2048, 1024)
    wo = np.concatenate([w_out[0:1024].reshape(16, 64, 2048)[heads].reshape(1024, 2048), w_out[1024:]], 0)
    tsc = []
    for n in ("ts_prev", "ts_next"):
        v = g[n][0]
        tsc.append(np.concatenate([columns(v[0:3328]), v[3328:3456][:, None], v[3360:3488][:, None]], 1))
    cc = np.stack([columns(g["c"][0]), columns(g["c_ctx"])], 2).reshape(128, 32)
    val = dict(sel=tab["sel"], ident=tab["ident"], ones=tab["ones"], blk=tab["blk"], rot32=tab["rot32"], rot128=tab["rot128"], c=cc,
               ada_b=columns(g["ada_b"][0]), norm1=columns(g["norm1_g"][0]), norm2=columns(g["norm2_g"][0]),
               final1=columns(g["final_norm_g"]), norm_a=columns(g["norm_a_2"][0]), norm_b=columns(g["norm_b_2"][0]),
               mem_g=columns(g["mem_norm_g_2"]), kv_g=columns(g["kv_norm_g_2"]), final2=columns(g["final_norm_g_2"]),
               ts=np.concatenate(tsc, 1), a0=np.concatenate([columns(g["a0"][0, d]) for d in range(2)], 1),
               k_k=columns(g["k_k"][0]), k_a=columns(g["k_a"][0]), r_k=columns(g["r_k"][0]), lnx_g=columns(g["lnx_g"][0]),
               lnx_b=columns(g["lnx_b"][0]), sink=np.broadcast_to(g["attn_sink"][0][heads][None, :], (128, 16)))
    fmaj = lambda a: np.ascontiguousarray(a.T.reshape(16, 128, T).transpose(1, 0, 2))
    gd = w_in[:, 4864:5024].reshape(4, 4, 128, 160).transpose(0, 2, 1, 3)
    arrays = dict(
        consts=np.concatenate([val[n] for n in COLS], 1), xT=fmaj(g["x"][0]), ctxT=fmaj(g["ctx"][0]), memT=fmaj(g["mem_2"][0]),
        ada=tiled(g["ada_w"][0]), w_q=tiled(wq), w_ka=tiled(w_in[:, 1024:1280]), w_va=tiled(w_in[:, 1280:1536]),
        w_r=tiled(w_in[:, 1536:2560]), w_k=tiled(w_in[:, 2560:3584]), w_v=tiled(w_in[:, 3584:4608]),
        w_wa=tiled(w_in[:, 4608:4864]), w_gd=gd, w_out=tiled(wo), ffn1=tiled(g["ffn_w1"][0]), ffn3=tiled(g["ffn_w3"][0]),
        ffn2=tiled(g["ffn_w2"][0]), w_in_a=tiled(g["w_in_a_2"][0]), w_out_a=tiled(g["w_out_a_2"][0]),
        w_in_b=tiled(g["w_in_b_2"][0]), w_out_b=tiled(g["w_out_b_2"][0]), mem0=tiled(g["w_mem_kv_2"][0]),
        mem1=tiled(g["w_mem_kv_2"][1]), w_kv=tiled(g["w_kv_2"]), w_up=g["w_up"][0].reshape(128, 1024),
        a_up=g["a_up"][0].reshape(128, 1024), w0=np.repeat(g["w0"][0], 64, axis=0), g_up=g["g_up"][0], attn_c=tab["attn_c"], ret_c=tab["ret_c"],
        decay=tab["decay"], dil_c=tab["dil_c"], rwkv_c=tab["rwkv_c"])
    nc = _bacc.Bacc("TRN2", target_bir_lowering=False, num_devices=1)
    io, feed = {}, {}
    for name, a in arrays.items():
        a = np.ascontiguousarray(a)
        feed[f"in_{name}"] = a
        io[name] = nc.dram_tensor(f"in_{name}", a.shape, mybir.dt.from_np(a.dtype), kind="ExternalInput").ap()
    io["mem_keep"] = nc.dram_tensor("mem_keep", (2, 8, 128, 512), F32, kind="Internal").ap()
    io["mix_keep"] = nc.dram_tensor("mix_keep", (128, 8, T), F32, kind="Internal").ap()
    io["x_keep"] = nc.dram_tensor("x_keep", (128, 16, T), F32, kind="Internal").ap()
    out = nc.dram_tensor("out_0", (128, 16, T), F32, kind="ExternalOutput").ap()
    bass_program(nc, io, out)
    r = _run(nc, [feed], core_ids=[0])
    y = np.asarray(r.results[0]["out_0"])
    return np.ascontiguousarray(y.transpose(2, 1, 0).reshape(1, T, 2048))
```
